# Optimizing a Trainium2 kernel written in Bass

```python
import jax
import jax.numpy as jnp
from jax import lax
import numpy as np

D_MODEL = 1024
BATCH = 1
SEQ = 1024
DEPTH = 1

D_MIX = D_MODEL
HEAD_DIM = 64
FOX_DIM = 3 * D_MIX // 8
HGRN_DIM = 3 * D_MIX // 8
POOL_DIM = D_MIX - FOX_DIM - HGRN_DIM
FOX_HEADS = FOX_DIM // HEAD_DIM
HGRN_HEADS = HGRN_DIM // HEAD_DIM
POOL_WINDOWS = (2, 4, 8, 16)
POOL_GROUPS = len(POOL_WINDOWS)
POOL_GROUP_DIM = POOL_DIM // POOL_GROUPS
Q_BLOCK = 128
HGRN_CHUNK = 64
N_EXPERT_GROUPS = 4
EXPERTS_PER_GROUP = 4
N_EXPERTS = N_EXPERT_GROUPS * EXPERTS_PER_GROUP
TOP_K = 2
D_FF_EXPERT = D_MODEL // 2
N_MOD = 6
EPS = 1e-6
PROJ_SPLITS = (FOX_DIM, FOX_DIM, FOX_DIM, FOX_HEADS,
               HGRN_DIM, HGRN_DIM, HGRN_DIM, HGRN_DIM, POOL_DIM)
PROJ_DIM = sum(PROJ_SPLITS)

kernel_name = 'hybrid_fox_hgrn2_pool_hmoe_adaln'

def rms_norm(x, gain):
    xf = x.astype(jnp.float32)
    y = xf * lax.rsqrt(jnp.mean(xf * xf, axis=-1, keepdims=True) + EPS)
    return (y * gain.astype(jnp.float32)).astype(x.dtype)

def head_rms_norm(x, gain):
    H, Dh = x.shape[-2], x.shape[-1]
    return rms_norm(x, gain.reshape(H, Dh))

def modulate(h, shift, scale):
    return h * (1 + scale) + shift

def split_heads(t, n_heads):
    B, S, _ = t.shape
    return t.reshape(B, S, n_heads, -1).transpose(0, 2, 1, 3)

def fox_attention(q, k, v, log_f):
    B, H, S, Dh = q.shape
    F = jnp.cumsum(log_f, axis=-1)
    scale = Dh ** -0.5
    neg = jnp.finfo(jnp.float32).min
    outs = []
    for blk in range(S // Q_BLOCK):
        lo, hi = blk * Q_BLOCK, (blk + 1) * Q_BLOCK
        qb = q[:, :, lo:hi]
        kb = k[:, :, :hi]
        vb = v[:, :, :hi]
        logits = jnp.einsum('bhqd,bhkd->bhqk', qb, kb).astype(jnp.float32) * scale
        logits = logits + F[:, :, lo:hi, None] - F[:, :, None, :hi]
        mask = (lo + jnp.arange(Q_BLOCK))[:, None] >= jnp.arange(hi)[None, :]
        logits = jnp.where(mask, logits, neg)
        p = jax.nn.softmax(logits, axis=-1)
        outs.append(jnp.einsum('bhqk,bhkd->bhqd', p.astype(v.dtype), vb))
    return jnp.concatenate(outs, axis=2)

def hgrn2_chunkwise(q, k, v, log_f):
    B, H, S, Dk = q.shape
    Dv = v.shape[-1]
    C = HGRN_CHUNK
    N = S // C

    def to_chunks(t):
        return t.astype(jnp.float32).reshape(B, H, N, C, t.shape[-1]).transpose(2, 0, 1, 3, 4)

    qc, kc, vc, gc = to_chunks(q), to_chunks(k), to_chunks(v), to_chunks(log_f)
    causal = jnp.tril(jnp.ones((C, C), dtype=bool))[:, :, None]

    def step(state, inp):
        qi, ki, vi, gi = inp
        b = jnp.cumsum(gi, axis=2)
        rel = b[:, :, :, None, :] - b[:, :, None, :, :]
        decay = jnp.exp(jnp.where(causal, rel, -jnp.inf))
        scores = jnp.einsum('bhtd,bhsd,bhtsd->bhts', qi, ki, decay)
        o_intra = jnp.einsum('bhts,bhse->bhte', scores, vi)
        o_inter = jnp.einsum('bhtd,bhde->bhte', qi * jnp.exp(b), state)
        b_last = b[:, :, -1:, :]
        k_dec = ki * jnp.exp(b_last - b)
        new_state = jnp.exp(b_last[:, :, 0, :])[..., None] * state + jnp.einsum('bhsd,bhse->bhde', k_dec, vi)
        return new_state, o_intra + o_inter

    state0 = jnp.zeros((B, H, Dk, Dv), jnp.float32)
    _, oc = lax.scan(step, state0, (qc, kc, vc, gc))
    return oc.transpose(1, 2, 0, 3, 4).reshape(B, H, S, Dv).astype(v.dtype)

def causal_multiscale_pool(u):
    B, S, _ = u.shape
    uf = u.astype(jnp.float32).reshape(B, S, POOL_GROUPS, POOL_GROUP_DIM)
    cs = jnp.concatenate([jnp.zeros((B, 1, POOL_GROUPS, POOL_GROUP_DIM), jnp.float32),
                          jnp.cumsum(uf, axis=1)], axis=1)
    pos = jnp.arange(S)
    means = []
    for g, w in enumerate(POOL_WINDOWS):
        start = jnp.maximum(pos + 1 - w, 0)
        window_sum = cs[:, 1:, g] - cs[:, start, g]
        count = (pos + 1 - start).astype(jnp.float32)
        means.append(window_sum / count[None, :, None])
    mean = jnp.stack(means, axis=2)
    return (mean - uf).astype(u.dtype)

def parallel_mixer(h, w_in, fox_f_bias, fox_norm_g, lower_bound, hgrn_norm_g, pool_w, pool_scale, w_out):
    B, S, _ = h.shape
    proj = h @ w_in
    offsets = []
    acc = 0
    for size in PROJ_SPLITS[:-1]:
        acc += size
        offsets.append(acc)
    fq, fk, fv, ff, hq, hf, hi, hg, pu = jnp.split(proj, offsets, axis=-1)

    log_fox = jax.nn.log_sigmoid(ff.astype(jnp.float32) + fox_f_bias.astype(jnp.float32))
    o_fox = fox_attention(split_heads(fq, FOX_HEADS), split_heads(fk, FOX_HEADS),
                          split_heads(fv, FOX_HEADS), log_fox.transpose(0, 2, 1))
    o_fox = head_rms_norm(o_fox.transpose(0, 2, 1, 3), fox_norm_g).reshape(B, S, FOX_DIM)

    f = lower_bound + (1 - lower_bound) * jax.nn.sigmoid(hf.astype(jnp.float32))
    o_hgrn = hgrn2_chunkwise(split_heads(jax.nn.silu(hq), HGRN_HEADS), split_heads(1 - f, HGRN_HEADS),
                             split_heads(hi, HGRN_HEADS), split_heads(jnp.log(f), HGRN_HEADS))
    o_hgrn = head_rms_norm(o_hgrn.transpose(0, 2, 1, 3), hgrn_norm_g).reshape(B, S, HGRN_DIM)
    o_hgrn = o_hgrn * jax.nn.silu(hg)

    pooled = causal_multiscale_pool(pu)
    o_pool = jnp.einsum('bsgc,gcd->bsgd', pooled, pool_w).reshape(B, S, POOL_DIM) * pool_scale

    merged = jnp.concatenate([o_fox.astype(h.dtype), o_hgrn.astype(h.dtype), o_pool.astype(h.dtype)], axis=-1)
    return merged @ w_out

def hierarchical_moe(h, w_rg, b_rg, w_re, b_re, w_gate, w_up, w_down):
    B, S, D = h.shape
    t = h.reshape(B * S, D)
    T = t.shape[0]
    group_logits = (t @ w_rg + b_rg).astype(jnp.float32)
    group_prob = jax.nn.softmax(group_logits, axis=-1)
    g_sel = jnp.argmax(group_logits, axis=-1)
    p_group = jnp.take_along_axis(group_prob, g_sel[:, None], axis=-1)
    expert_logits = (t @ w_re + b_re).astype(jnp.float32).reshape(T, N_EXPERT_GROUPS, EXPERTS_PER_GROUP)
    local_logits = jnp.take_along_axis(expert_logits, g_sel[:, None, None], axis=1)[:, 0]
    local_prob = jax.nn.softmax(local_logits, axis=-1)
    top_p, top_i = lax.top_k(local_prob, TOP_K)
    top_w = top_p / jnp.sum(top_p, axis=-1, keepdims=True) * p_group
    expert_id = g_sel[:, None] * EXPERTS_PER_GROUP + top_i
    combine = jnp.sum(jax.nn.one_hot(expert_id, N_EXPERTS, dtype=jnp.float32) * top_w[..., None], axis=1)

    def expert_step(acc, inp):
        wg, wu, wd, cw = inp
        hidden = jax.nn.silu(t @ wg) * (t @ wu)
        return acc + cw[:, None].astype(t.dtype) * (hidden @ wd), None

    out, _ = lax.scan(expert_step, jnp.zeros_like(t), (w_gate, w_up, w_down, combine.T))
    return out.reshape(B, S, D)

def setup_inputs(seed: int = 0) -> dict:
    key = jax.random.key(seed)
    ks = jax.random.split(key, 24)

    def nrm(k, shape, scale):
        return jax.random.normal(k, shape, jnp.float32) * scale

    D, E, F = D_MODEL, N_EXPERTS, D_FF_EXPERT
    return {
        'x': nrm(ks[0], (BATCH, SEQ, D), 1.0),
        'c': nrm(ks[1], (BATCH, D), 1.0),
        'w_ada': nrm(ks[2], (DEPTH, D, N_MOD * D), 0.1 * D ** -0.5),
        'b_ada': nrm(ks[3], (DEPTH, N_MOD * D), 0.02),
        'norm1_g': 1.0 + nrm(ks[4], (DEPTH, D), 0.05),
        'w_in': nrm(ks[5], (DEPTH, D, PROJ_DIM), D ** -0.5),
        'fox_f_bias': jax.random.uniform(ks[6], (DEPTH, FOX_HEADS), jnp.float32, 1.0, 5.0),
        'fox_norm_g': 1.0 + nrm(ks[7], (DEPTH, FOX_DIM), 0.05),
        'hgrn_lb_logits': nrm(ks[8], (DEPTH, HGRN_DIM), 0.1),
        'hgrn_norm_g': 1.0 + nrm(ks[9], (DEPTH, HGRN_DIM), 0.05),
        'pool_w': nrm(ks[10], (DEPTH, POOL_GROUPS, POOL_GROUP_DIM, POOL_GROUP_DIM), POOL_GROUP_DIM ** -0.5),
        'pool_scale': 1.0 + nrm(ks[11], (DEPTH, POOL_DIM), 0.05),
        'w_out': nrm(ks[12], (DEPTH, D_MIX, D), D_MIX ** -0.5),
        'norm2_g': 1.0 + nrm(ks[13], (DEPTH, D), 0.05),
        'router_group_w': nrm(ks[14], (DEPTH, D, N_EXPERT_GROUPS), D ** -0.5),
        'router_group_b': nrm(ks[15], (DEPTH, N_EXPERT_GROUPS), 0.01),
        'router_expert_w': nrm(ks[16], (DEPTH, D, E), D ** -0.5),
        'router_expert_b': nrm(ks[17], (DEPTH, E), 0.01),
        'expert_w_gate': nrm(ks[18], (DEPTH, E, D, F), D ** -0.5),
        'expert_w_up': nrm(ks[19], (DEPTH, E, D, F), D ** -0.5),
        'expert_w_down': nrm(ks[20], (DEPTH, E, F, D), F ** -0.5),
        'final_norm_g': 1.0 + nrm(ks[21], (D,), 0.05),
    }

def reference(x, c, w_ada, b_ada, norm1_g, w_in, fox_f_bias, fox_norm_g, hgrn_lb_logits, hgrn_norm_g,
              pool_w, pool_scale, w_out, norm2_g, router_group_w, router_group_b, router_expert_w,
              router_expert_b, expert_w_gate, expert_w_up, expert_w_down, final_norm_g):
    mod_all = jnp.einsum('bd,lde->lbe', jax.nn.silu(c), w_ada) + b_ada[:, None, :]
    lb_cum = jnp.cumsum(jax.nn.softmax(hgrn_lb_logits.astype(jnp.float32), axis=0), axis=0)
    lower_bounds = lb_cum - lb_cum[0:1]
    for l in range(DEPTH):
        shift1, scale1, gate1, shift2, scale2, gate2 = jnp.split(mod_all[l][:, None, :], N_MOD, axis=-1)
        h = modulate(rms_norm(x, norm1_g[l]), shift1, scale1)
        y = parallel_mixer(h, w_in[l], fox_f_bias[l], fox_norm_g[l], lower_bounds[l], hgrn_norm_g[l],
                           pool_w[l], pool_scale[l], w_out[l])
        x = x + (1 + gate1) * y
        h = modulate(rms_norm(x, norm2_g[l]), shift2, scale2)
        y = hierarchical_moe(h, router_group_w[l], router_group_b[l], router_expert_w[l], router_expert_b[l],
                             expert_w_gate[l], expert_w_up[l], expert_w_down[l])
        x = x + (1 + gate2) * y
    return rms_norm(x, final_norm_g)


_drawn_inputs = setup_inputs


def setup_inputs(seed=0):
    import zlib

    import numpy as np

    out = dict(_drawn_inputs(seed))
    spreads = {}
    factors = {'router_group_b': 47.992, 'router_expert_b': 7.903}
    for name, (base, spread) in spreads.items():
        noise = np.random.default_rng([zlib.crc32(name.encode()), seed]).standard_normal(out[name].shape)
        drawn = base * np.exp(spread * noise) if base else spread * noise
        out[name] = jnp.asarray(drawn.astype(out[name].dtype))
    for name, factor in factors.items():
        out[name] = (out[name] * factor).astype(out[name].dtype)
    return out
```

```python
from contextlib import ExitStack

import concourse.bass as bass
from concourse import mybir

F32 = mybir.dt.float32
I32 = mybir.dt.int32
U32 = mybir.dt.uint32
ALU = mybir.AluOpType
ACT = mybir.ActivationFunctionType
AX = mybir.AxisListType

P = 128
D = 1024
S = 1024
K = D // P
T = S // P
HD = 64
FOX = 384
HG = 384
PL = 256
NH = FOX // HD
PAIRS = NH // 2
MOD_N = 6
CH = 512
E_ALL = 16
G = 4
EG = 4
FF = 512
FC = FF // P
EPS = 1e-6
TILES = 32
LEVELS = 7
HALF = S // 2

AT_FQ, AT_FK, AT_FV, AT_HQ, AT_HF, AT_HI, AT_HG, AT_PU = 0, 384, 768, 1158, 1542, 1926, 2310, 2694
VW = FOX + NH
B_FQ, B_HQ, B_PU, B_FK, B_HF, B_HG = 0, 3, 6, 8, 11, 14
BLOCK_COLUMNS = ([AT_FQ + P * j for j in range(3)] + [AT_HQ + P * j for j in range(3)]
                 + [AT_PU + P * j for j in range(2)] + [AT_FK + P * j for j in range(3)]
                 + [AT_HF + P * j for j in range(3)] + [AT_HG + P * j for j in range(3)])
NB = len(BLOCK_COLUMNS)


class Chain:

    def __init__(self, eng, sem):
        self.eng, self.sem, self.n, self.base = eng, sem, 0, 0

    def __call__(self, ins):
        self.n += 1
        ins.then_inc(self.sem, 1)
        self.eng.wait_ge(self.sem, self.n + self.base)

    def enter(self, i, per):
        self.kept, self.per = self.n, per
        self.base = i * per

    def leave(self, times):
        assert self.n - self.kept == self.per, (self.n - self.kept, self.per)
        self.n, self.base = self.kept + self.per * times, 0


def copied_b(n):
    return n // 8 * 4 + max(n % 8 - 3, 0)


def build(nc, a, out):
    f2 = lambda ap: ap.rearrange("a d -> (a d)")

    x_v = a["x"][0].rearrange("(t p) d -> p t d", p=P)
    out_v = out[0].rearrange("(t p) d -> p t d", p=P)
    c_v = a["c"].rearrange("b (p k) -> p (b k)", k=K)
    ada_v = a["w_ada"][0].rearrange("(p k) (n e) -> n p k e", k=K, e=CH)
    win_v = a["w_in"][0].rearrange("(k p) n -> p k n", p=P)
    wout_v = a["w_out"][0].rearrange("(k p) n -> p k n", p=P)
    wg_v = a["expert_w_gate"][0].rearrange("e (k p) f -> e p k f", p=P)
    wu_v = a["expert_w_up"][0].rearrange("e (k p) f -> e p k f", p=P)
    wd_v = a["expert_w_down"][0].rearrange("e (k p) f -> e p k f", p=P)
    col = lambda ap: ap.rearrange("a (n p) -> p (a n)", p=P)

    f_rows = nc.dram_tensor("f_rows", [2, NH, S], F32, kind="Internal").ap()
    h2_rows = nc.dram_tensor("h2_rows", [S, D], F32, kind="Internal").ap()
    y_rows = nc.dram_tensor("y_rows", [TILES * P, D], F32, kind="Internal").ap()
    slot_token = nc.dram_tensor("slot_token", [TILES * P, 1], U32, kind="Internal").ap()

    with ExitStack() as ctx:
        at = [16512]

        def put(name, shape, dt=F32, offset=None):
            size = 4
            for n in shape[1:]:
                size *= n
            o = offset
            if o is None:
                o = at[0]
                at[0] = (o + size + 31) // 32 * 32
            return nc.alloc_sbuf_tensor_at(name, shape, dt, offset=o)

        ident = put("ident", [P, P])
        ones = put("ones", [P, P])
        before = put("before", [P, P])
        causal = put("causal", [P, P])
        level_mask = put("level_mask", [P, LEVELS, P])
        c_raw = put("c_raw", [P, K])
        c_silu = put("c_silu", [P, K])
        waited = put("waited", [P, 16])
        waited_pool = put("waited_pool", [P, 2])
        ss = put("ss", [P, T])
        ms = put("ms", [P, T])
        rstd = put("rstd", [P, T])
        power = put("power", [P, 96])
        g1c = put("g1c", [P, K])
        scale1c = put("scale1c", [P, K])
        shift1c = put("shift1c", [P, K])
        foxg = put("foxg", [P, PAIRS])
        hgrng = put("hgrng", [P, PAIRS])
        lbl = put("lbl", [P, PAIRS])
        lbd = put("lbd", [P, PAIRS])
        lbe = put("lbe", [P, PAIRS])
        lbr = put("lbr", [P, PAIRS])
        lbp = put("lbp", [P, PAIRS])
        lb = put("lb", [P, PAIRS])
        oml = put("oml", [P, PAIRS])
        pscale = put("pscale", [P, 2])
        fbias = put("fbias", [P, NH])
        rbias = put("rbias", [P, G + E_ALL])
        gate = put("gate", [P, T, NH])
        gate_abs = put("gate_abs", [P, T, NH])
        gate_exp = put("gate_exp", [P, T, NH])
        gate_ln = put("gate_ln", [P, T, NH])
        log_forget = put("log_forget", [P, T, NH])
        nmax = put("nmax", [P, 2])
        pool_w = put("pool_w", [P, 2, P])
        wcol = put("wcol", [P, 2])
        iwcol = put("iwcol", [P, 2])
        invc = put("invc", [P, 2, 16])
        head_ss = put("head_ss", [P, 2, T * NH])
        head_ms = put("head_ms", [P, 2, T * NH])
        head_r = put("head_r", [P, 2, T * NH])
        rl = put("rl", [P, T * NH])
        el = put("el", [P, T])
        states = put("states", [P, T, HD])
        rw = put("rw", [P, K, G + E_ALL])
        logits = put("logits", [P, T, G + E_ALL])
        X = put("X", [P, T, D])
        mod = put("mod", [P, 2 * MOD_N, CH])
        mod_at = at[0] - 2 * MOD_N * CH * 4
        pt_at = at[0]
        PT = put("PT", [P, NB, S])
        va_at = at[0]
        VA = put("VA", [P, T, NH, HD + 1])
        HI = put("HI", [P, T, HG])
        r_at = at[0]
        end = 229344
        assert r_at + 45248 <= end, (r_at, end)
        ada = put("ada", [P, 2, K, CH], offset=pt_at)
        xhat = put("xhat", [P, T, D], offset=pt_at + 32768)
        junk = put("junk", [P, D], offset=pt_at + 65536)
        c_wide = put("c_wide", [P, K, P], offset=r_at + 32768)
        hT = put("hT", [P, K, S], offset=r_at)
        w_v = put("w_v", [P, K, VW], offset=pt_at)
        w_i = put("w_i", [P, K, HG], offset=pt_at + 4 * K * VW)
        w_t = put("w_t", [P, 3, K, P], offset=r_at + 32768)
        QA = [put(f"QA{e}", [HD + 2, S], offset=r_at + 8192 * e) for e in range(2)]
        KA = [put(f"KA{e}", [HD + 2, S], offset=r_at + 8192 * e + 4096) for e in range(2)]
        prob = put("prob", [P, 2, S], offset=r_at + 16384)
        probT = put("probT", [P, 2, T, P], offset=r_at + 24576)
        OF = put("OF", [P, T, NH, HD + 1], offset=r_at + 32768)
        f_sum = put("f_sum", [NH, S], offset=r_at + 16384)
        f_neg = put("f_neg", [NH, S], offset=r_at + 20480)
        ones_row = put("ones_row", [NH, S], offset=r_at + 24576)
        win_sum = put("win_sum", [P, 2, S], offset=mod_at)
        qb = put("qb", [P, S], offset=r_at)
        kb = put("kb", [P, S], offset=r_at + 4096)
        bsum = put("bsum", [P, S], offset=r_at + 8192)
        dec = put("dec", [P, 2, S], offset=r_at + 12288)
        gk = put("gk", [P, 2, S], offset=r_at + 20480)
        qe = put("qe", [P, S], offset=r_at + 28672)
        scores = put("scores", [P, 2, T, P], offset=pt_at + B_FK * 4096)
        carry = put("carry", [P, S], offset=pt_at + (B_FK + 2) * 4096)
        kdT = put("kdT", [P, T, P], offset=mod_at)
        HO = put("HO", [P, T, NH, HD], offset=va_at)
        sq = put("sq", [P, T, NH, HD], offset=r_at)
        ON = put("ON", [P, T, NH, HD], offset=r_at + 12288)
        wo_a = put("wo_a", [P, 6, D], offset=pt_at + B_FK * 4096)
        wo_b = put("wo_b", [P, 2, D], offset=mod_at)
        ytmp = put("ytmp", [P, 2, D], offset=r_at)
        h2 = put("h2", [P, 2, D], offset=r_at + 8192)
        h2T = put("h2T", [P, 2, K, P], offset=r_at + 16384)
        junk2 = put("junk2", [P, D], offset=r_at + 24576)
        g2 = put("g2", [P, D], offset=r_at + 40960)
        rt_at = [r_at]

        def small(name, shape, dt=F32):
            size = 4
            for n in shape[1:]:
                size *= n
            o = rt_at[0]
            rt_at[0] += (size + 31) // 32 * 32
            return put(name, shape, dt, offset=o)

        first4 = small("first4", [P, EG])
        gmax = small("gmax", [P, T])
        gdif = small("gdif", [P, T, G])
        gexp = small("gexp", [P, T, G])
        gsum = small("gsum", [P, T])
        pgroup = small("pgroup", [P, T])
        eqv = small("eqv", [P, T, 4])
        fst = small("fst", [P, T])
        oh_g = small("oh_g", [P, T, G])
        picked = small("picked", [P, T, EG, G])
        local = small("local", [P, T, EG])
        lmax = small("lmax", [P, T])
        oh_1 = small("oh_1", [P, T, EG])
        local2 = small("local2", [P, T, EG])
        lmax2 = small("lmax2", [P, T])
        oh_2 = small("oh_2", [P, T, EG])
        ldif = small("ldif", [P, T])
        lexp = small("lexp", [P, T])
        lden = small("lden", [P, T])
        lrec = small("lrec", [P, T])
        m1 = small("m1", [P, T, G, EG])
        m2 = small("m2", [P, T, G, EG])
        both = small("both", [P, T, E_ALL])
        rank = small("rank", [P, T, E_ALL])
        tot = small("tot", [P, T, E_ALL])
        run = small("run", [P, T + 1, E_ALL])
        hund = small("hund", [P, E_ALL, T])
        ntile = small("ntile", [P, E_ALL])
        tend = small("tend", [P, E_ALL])
        tbase = small("tbase", [P, E_ALL])
        pos = small("pos", [P, T, E_ALL])
        pick = small("pick", [P, T, E_ALL])
        slots = small("slots", [P, 2, T])
        step128 = small("step128", [P, T])
        tile_no = small("tile_no", [P, TILES])
        t_cmp = small("t_cmp", [P, TILES, E_ALL])
        t_exp = small("t_exp", [P, TILES])
        token_id = small("token_id", [P, T], U32)
        zero_slots = small("zero_slots", [P, TILES], U32)
        assert rt_at[0] <= r_at + 40960, rt_at[0] - r_at
        w12 = put("w12", [P, 2, T], offset=end - 64)
        slots_i = put("slots_i", [P, 2, T], U32, offset=end - 128)
        t_exp_i = put("t_exp_i", [P, TILES], I32, offset=end - 256)
        mo = pt_at
        wg = put("wg", [P, 2, K, FF], offset=mo)
        wu = put("wu", [P, 2, K, FF], offset=mo + 32768)
        wd = put("wd", [P, 2, FC, D], offset=mo + 65536)
        XG = put("XG", [P, 2, D], offset=mo + 98304)
        XT = put("XT", [P, 2, K, P], offset=mo + 106496)
        sil = put("sil", [P, FF], offset=mo + 114688)
        hid = put("hid", [P, FF], offset=mo + 116736)
        hidT = put("hidT", [P, FC, P], offset=mo + 118784)
        Y = put("Y", [P, 2, D], offset=mo + 120832)
        tok = put("tok", [P, 2], U32, offset=mo + 129024)
        assert mo + 129032 < end - 256 - 4096
        ya = put("ya", [P, 2, D], offset=mo)
        yb = put("yb", [P, 2, D], offset=mo + 8192)
        fin = put("fin", [P, 2, D], offset=mo + 16384)
        junk3 = put("junk3", [P, D], offset=mo + 24576)
        gf = put("gf", [P, D], offset=mo + 28672)

        PS = ctx.enter_context(nc.psum_tensor("PS", [P, 8, 512], F32))

        def sem(name):
            return ctx.enter_context(nc.semaphore(name))

        dve_step, pool_step, act_step = sem("dve_step"), sem("pool_step"), sem("act_step")
        (c_in, x_in, small_in, bada_in, win_v_in, rows_out, rows_in) = map(sem, (
            "c_in", "x_in", "small_in", "bada_in", "win_v_in", "rows_out", "rows_in"))
        ada_in = [sem(f"ada_in{s}") for s in range(2)]
        win_in = [sem(f"win_in{s}") for s in range(3)]
        (consts, silu_c, c_wide_up, ada_mm, ada_out, x_sq, x_hat, cols_mm, cols_up, tx_done,
         ht_act, ht_dve) = map(sem, (
            "consts", "silu_c", "c_wide_up", "ada_mm", "ada_out", "x_sq", "x_hat", "cols_mm",
            "cols_up", "tx_done", "ht_act", "ht_dve"))
        v_mm, va_out, hi_out, proj_mm, pt_act, pt_dve = map(sem, (
            "v_mm", "va_out", "hi_out", "proj_mm", "pt_act", "pt_dve"))
        (gate_up, gate_ln_up, lf_up, lf_T, f_up, silu_up, q_scaled, pooled_up,
         mod_up) = map(sem, (
            "gate_up", "gate_ln_up", "lf_up", "lf_T", "f_up", "silu_up", "q_scaled", "pooled_up",
            "mod_up"))
        qk_in = [sem(f"qk_in{e}") for e in range(2)]
        s_done, max_up, p_up, t_done, pta, ptb, pv_done, o_out = map(sem, (
            "s_done", "max_up", "p_up", "t_done", "pta", "ptb", "pv_done", "o_out"))
        (k_up, logf_up, b_up, q_up, qe_exp, qe_up, kd_d, kd_e, kd_up, kdT_mm, kdT_up, ds_mm, st_up,
         d_up, e_up, g_up, lv_mm, sc_out, ho_mm, ho_out) = map(sem, (
            "k_up", "logf_up", "b_up", "q_up", "qe_exp", "qe_up", "kd_d", "kd_e", "kd_up",
            "kdT_mm", "kdT_up", "ds_mm", "st_up", "d_up", "e_up", "g_up", "lv_mm", "sc_out",
            "ho_mm", "ho_out"))
        pool_mm, pool_out, fsq_in, fsq, fss, frs, on_up, mT_mm, mT_act, mT_dve, wo_in = map(sem, (
            "pool_mm", "pool_out", "fsq_in", "fsq", "fss", "frs", "on_up", "mT_mm", "mT_act",
            "mT_dve", "wo_in"))
        (y_mm, y_gated, x2_up, x2_sq, h2_r, h2_m, h2_up, h2_T, h2T_up, rt_mm, rt_out,
         g2_in) = map(sem, (
            "y_mm", "y_gated", "x2_up", "x2_sq", "h2_r", "h2_m", "h2_up", "h2_T",
            "h2T_up", "rt_mm", "rt_out", "g2_in"))
        (r_exp_in, r_exp, masks_up, rank_mm, slots_up, zeros_out, slots_out, iota_up) = map(sem, (
            "r_exp_in", "r_exp", "masks_up", "rank_mm", "slots_up", "zeros_out", "slots_out",
            "iota_up"))
        h2_out = [sem(f"h2_out{s}") for s in range(2)]
        gu_in = [sem(f"gu_in{s}") for s in range(2)]
        d_in = [sem(f"d_in{s}") for s in range(2)]
        tok_in = [sem(f"tok_in{s}") for s in range(2)]
        xg_in = [sem(f"xg_in{s}") for s in range(2)]
        y_out = [sem(f"y_out{s}") for s in range(2)]
        (xT_mm, xT_act, xT_dve, g_mm, u_mm, sil_up, hid_up, hT_mm, hT_up, dn_mm, y_act,
         y_dve) = map(sem, (
            "xT_mm", "xT_act", "xT_dve", "g_mm", "u_mm", "sil_up", "hid_up", "hT_mm", "hT_up",
            "dn_mm", "y_act", "y_dve"))
        ya_in = [sem(f"ya_in{s}") for s in range(2)]
        yb_in = [sem(f"yb_in{s}") for s in range(2)]
        fin_out = [sem(f"fin_out{s}") for s in range(2)]
        tok_seen = sem("tok_seen")
        gf_in, x3_sq, x3_up, x3_r, fin_up = map(sem, ("gf_in", "x3_sq", "x3_up", "x3_r", "fin_up"))

        N_SMALL = 14
        FINI = 2 * PAIRS * 2

        def tokens(t):
            return slice(t * P, (t + 1) * P)

        def heads(ap):
            return ap.rearrange("p t h d -> p (t h) d")

        block = ctx.enter_context(nc.Block())

        @block.sync
        def _(sp):
            sp.dma_start(c_raw[:], c_v).then_inc(c_in, 16)
            for s in range(2):
                sp.dma_start(ada[:, s], ada_v[s]).then_inc(ada_in[s], 16)
            sp.dma_start(X[:, 0:4], x_v[:, 0:4]).then_inc(x_in, 16)
            with sp.Fori(1, MOD_N) as i:
                for s in range(2):
                    sp.wait_ge(ada_mm, 2 * i - 1 + s)
                    sp.dma_start(ada[:, s], ada_v[2 * i + s]).then_inc(ada_in[s], 16)
            sp.wait_ge(ada_mm, 2 * MOD_N)
            sp.dma_start(w_v[:], win_v[:, :, AT_FV:AT_FV + VW]).then_inc(win_v_in, 16)
            sp.dma_start(w_i[:], win_v[:, :, AT_HI:AT_HI + HG]).then_inc(win_v_in, 16)
            for b, c0 in enumerate(BLOCK_COLUMNS):
                if b >= 3:
                    sp.wait_ge(proj_mm, 2 * b - 4)
                sp.dma_start(w_t[:, b % 3], win_v[:, :, c0:c0 + P]).then_inc(win_in[b % 3], 16)
            sp.wait_ge(f_up, 2)
            sp.dma_start(f_rows[0], f_sum[:]).then_inc(rows_out, 16)
            sp.dma_start(f_rows[1], f_neg[:]).then_inc(rows_out, 16)
            sp.wait_ge(rows_out, 32)
            sp.wait_ge(q_scaled, 4)

            def load_pair(i, first):
                for e in range(2):
                    if not first:
                        sp.wait_ge(s_done, 16 * i - 8 + 8 * e)
                    half = slice(HD * e, HD * (e + 1))
                    sp.dma_start(QA[e][0:HD, :], PT[half, B_FQ + i, :]).then_inc(qk_in[e], 16)
                    sp.dma_start(KA[e][0:HD, :], PT[half, B_FK + i, :]).then_inc(qk_in[e], 16)
                    sp.dma_start(QA[e][HD + 1:HD + 2, :], f_rows[0, bass.ds(2 * i + e, 1), :])\
                        .then_inc(qk_in[e], 16)
                    sp.dma_start(KA[e][HD:HD + 1, :], f_rows[1, bass.ds(2 * i + e, 1), :])\
                        .then_inc(qk_in[e], 16)

            load_pair(0, True)
            with sp.Fori(1, PAIRS) as i:
                load_pair(i, False)
            sp.wait_ge(ho_mm, PAIRS)
            sp.dma_start(wo_a[:], wout_v[:, 0:6, :]).then_inc(wo_in, 16)
            sp.dma_start(wo_b[:], wout_v[:, 6:8, :]).then_inc(wo_in, 16)
            for t in range(T):
                sp.wait_ge(h2_up, t + 1)
                sp.dma_start(h2_rows[t * P:(t + 1) * P, :], h2[:, t % 2, :]).then_inc(h2_out[t % 2], 16)
            sp.wait_ge(slots_up, 1)
            sp.wait_ge(rt_mm, T)

            def load_expert(j, s, first):
                e = sp.value_load(t_exp_i[0:1, bass.ds(j, 1)], min_val=0, max_val=E_ALL - 1)
                if not first:
                    sp.wait_ge(u_mm, j - 1)
                sp.dma_start(wg[:, s], wg_v[e]).then_inc(gu_in[s], 16)
                sp.dma_start(wu[:, s], wu_v[e]).then_inc(gu_in[s], 16)
                if not first:
                    sp.wait_ge(dn_mm, 2 * j - 2)
                sp.dma_start(wd[:, s], wd_v[e]).then_inc(d_in[s], 16)

            for s in range(2):
                load_expert(s, s, True)
            with sp.Fori(1, TILES // 2) as i:
                for s in range(2):
                    load_expert(2 * i + s, s, False)
            for t in range(T):
                sp.wait_ge(fin_up, t + 1)
                sp.dma_start(out_v[:, t], fin[:, t % 2, :]).then_inc(fin_out[t % 2], 16)
            for s in range(2):
                sp.wait_ge(fin_out[s], 16 * T // 2)
            for s in range(2):
                sp.wait_ge(y_out[s], 16 * TILES // 2)

        @block.tensor
        def _(pe):
            mm, tr = nc.tensor.matmul, nc.tensor.transpose
            pe.wait_ge(c_wide_up, 1)

            def ada_chunks(i, first):
                for s in range(2):
                    pe.wait_ge(ada_in[s], 16 * i + 16)
                    if not first:
                        pe.wait_ge(ada_out, 2 * i - 1 + s)
                    for k in range(K):
                        m = mm(PS[:, s, :], c_wide[:, k, :], ada[:, s, k, :],
                               start=(k == 0), stop=(k == K - 1))
                    m.then_inc(ada_mm, 1)

            ada_chunks(0, True)
            with pe.Fori(1, MOD_N) as i:
                ada_chunks(i, False)
            pe.wait_ge(consts, 1)
            pe.wait_ge(ada_out, 2 * MOD_N)
            for j in range(4):
                for q in range(4):
                    n = 4 * j + q
                    m = mm(PS[:, 2, n:n + 1], mod[0:1, j, q * P:(q + 1) * P], ones[0:1, 0:1],
                           start=True, stop=True)
            m.then_inc(cols_mm, 1)
            pe.wait_ge(x_hat, T)
            for j in range(2 * K):
                if j == 2:
                    pe.wait_ge(cols_up, 2)
                if j >= 8:
                    pe.wait_ge([ht_act, ht_dve][j % 2], (j - 8) // 2 + 1)
                for q in range(4):
                    m = tr(PS[:, j % 8, q * P:(q + 1) * P],
                           xhat[:, 4 * (j % 2) + q, (j // 2) * P:(j // 2 + 1) * P], ident[:])
                m.then_inc(tx_done, 1)
            pe.wait_ge(ht_act, K)
            pe.wait_ge(ht_dve, K)
            pe.wait_ge(win_v_in, 32)
            for t in range(T):
                b = 2 * t % 8
                if t >= 4:
                    pe.wait_ge(va_out, t - 3)
                    pe.wait_ge(hi_out, t - 3)
                for k in range(K):
                    mm(PS[:, b, 0:VW], hT[:, k, tokens(t)], w_v[:, k, :],
                       start=(k == 0), stop=(k == K - 1))
                for k in range(K):
                    m = mm(PS[:, b + 1, 0:HG], hT[:, k, tokens(t)], w_i[:, k, :],
                           start=(k == 0), stop=(k == K - 1))
                m.then_inc(v_mm, 1)
            pe.wait_ge(va_out, T)
            pe.wait_ge(hi_out, T)

            def proj_block(s, turn, b):
                pe.wait_ge(win_in[s], 16 * turn + 16)
                if b is not None:
                    pe.wait_ge(pt_act, b - 2)
                    pe.wait_ge(pt_dve, b - 2)
                for h in range(2):
                    for k in range(K):
                        m = mm(PS[:, 2 * s + h, :], w_t[:, s, k, :],
                               hT[:, k, h * HALF:(h + 1) * HALF], start=(k == 0), stop=(k == K - 1))
                    m.then_inc(proj_mm, 1)

            for s in range(3):
                proj_block(s, 0, None)
            with pe.Fori(1, NB // 3) as i:
                for s in range(3):
                    proj_block(s, i, 3 * i + s)
            for s in range(NB % 3):
                proj_block(s, NB // 3, NB // 3 * 3 + s)
            pe.wait_ge(lf_up, 1)
            for t in range(T):
                m = tr(PS[0:NH, 6 + t // 4, (t % 4) * P:(t % 4 + 1) * P], log_forget[:, t, :],
                       ident[:])
            m.then_inc(lf_T, 1)

            def fox_scores(i, n, first):
                e, q = n // 8, n % 8
                if q == 0:
                    pe.wait_ge(qk_in[e], 64 * i + 64)
                if not first or n >= 2:
                    pe.wait_ge(p_up, 16 * i + n - 1)
                w = (q + 1) * P
                for c in range((w + 511) // 512):
                    u = min(w - 512 * c, 512)
                    m = mm(PS[:, n % 2 * 2 + c, 0:u], QA[e][:, tokens(q)],
                           KA[e][:, 512 * c:512 * c + u], start=True, stop=True)
                m.then_inc(s_done, 1)

            def fox_transpose(i, n, first):
                q = n % 8
                pe.wait_ge(p_up, 16 * i + n + 1)
                if not first or n >= 1:
                    pe.wait_ge(pta, 16 * i + n)
                    if not first or n >= 5:
                        pe.wait_ge(ptb, 8 * i + copied_b(n - 1))
                for k in range(q + 1):
                    m = tr(PS[:, 4 + k // 4, (k % 4) * P:(k % 4 + 1) * P],
                           prob[:, n % 2, tokens(k)], ident[:])
                m.then_inc(t_done, 1)

            def fox_values(i, n, first):
                e, q = n // 8, n % 8
                pe.wait_ge(pta, 16 * i + n + 1)
                if q >= 4:
                    pe.wait_ge(ptb, 8 * i + copied_b(n))
                if not first or n >= 2:
                    pe.wait_ge(o_out, 16 * i + n - 1)
                for k in range(q + 1):
                    m = mm(PS[:, 6 + n % 2, 0:HD + 1], probT[:, n % 2, k, :],
                           VA[:, k, 2 * i + e, :], start=(k == 0), stop=(k == q))
                m.then_inc(pv_done, 1)

            def fox_pair(i, first):
                for n in range(18):
                    if n < 16:
                        fox_scores(i, n, first)
                    if 1 <= n < 17:
                        fox_transpose(i, n - 1, first)
                    if n >= 2:
                        fox_values(i, n - 2, first)

            pe.wait_ge(f_up, 2)
            pe.wait_ge(consts, 1)
            fox_pair(0, True)
            with pe.Fori(1, PAIRS) as i:
                fox_pair(i, False)

            pe.wait_ge(pooled_up, 2)
            for b in range(2):
                for h in range(2):
                    m = mm(PS[:, 2 * b + h, :], pool_w[:, b, :],
                           PT[:, B_PU + b, h * HALF:(h + 1) * HALF], start=True, stop=True)
            m.then_inc(pool_mm, 1)
            pe.wait_ge(pool_out, 1)
            pe.wait_ge(o_out, 16 * PAIRS)

            def level_products(i, lv, lhs, rhs, first):
                for st in range(2):
                    r = 2 * lv + st
                    if not first or r >= 2:
                        pe.wait_ge(sc_out, 16 * i + r - 1)
                    for c in range(4):
                        for e in range(2):
                            half = slice(HD * e, HD * (e + 1))
                            tk = tokens(4 * st + c)
                            m = mm(PS[:, 2 * st + e, c * P:(c + 1) * P], lhs[half, tk],
                                   rhs[half, tk], start=True, stop=True)
                    m.then_inc(lv_mm, 1)

            def hgrn_pair(i, first):
                pe.wait_ge(k_up, i + 1)
                pe.wait_ge(q_up, i + 1)
                level_products(i, 0, kb, qb, first)
                pe.wait_ge(kd_up, i + 1)
                if not first:
                    pe.wait_ge(ho_out, i)
                for c in range(T):
                    m = tr(PS[:, 4 + c // 4, (c % 4) * P:(c % 4 + 1) * P], dec[:, 0, tokens(c)],
                           ident[:])
                m.then_inc(kdT_mm, 1)
                for lv in range(LEVELS):
                    pe.wait_ge(g_up, LEVELS * i + lv + 1)
                    g = gk[:, lv % 2, :]
                    level_products(i, lv + 1, g, g, first)
                    if lv == 0:
                        pe.wait_ge(kdT_up, i + 1)
                        for c in range(T):
                            m = mm(PS[:, 6 + c // 4, (c % 4) * P:(c % 4 + 1) * P], kdT[:, c, :],
                                   HI[:, c, bass.ds(P * i, P)], start=True, stop=True)
                        m.then_inc(ds_mm, 1)
                pe.wait_ge(qe_up, i + 1)
                pe.wait_ge(st_up, i + 1)
                pe.wait_ge(sc_out, 16 * i + 16)
                for c in range(T):
                    for e in range(2):
                        half = slice(HD * e, HD * (e + 1))
                        o = PS[:, 4 + e, c * HD:(c + 1) * HD]
                        m = mm(o, scores[:, e, c, :], HI[:, c, bass.ds(P * i + HD * e, HD)],
                               start=True, stop=(c == 0))
                        if c > 0:
                            m = mm(o, qe[half, tokens(c)], states[half, c, :], start=False,
                                   stop=True)
                m.then_inc(ho_mm, 1)

            hgrn_pair(0, True)
            with pe.Fori(1, PAIRS) as i:
                hgrn_pair(i, False)

            for j in range(2 * FINI // 2):
                g, r = j // (2 * PAIRS), j % (2 * PAIRS)
                src = (ON, HO)[g]
                if r == 0:
                    pe.wait_ge(on_up, g + 1)
                    if g == 0:
                        pe.wait_ge(ho_out, PAIRS)
                if j >= 8:
                    pe.wait_ge([mT_act, mT_dve][j % 2], (j - 8) // 2 + 1)
                for q in range(4):
                    t = 4 * (r % 2) + q
                    pair = r // 2
                    m = tr(PS[:, j % 8, q * P:(q + 1) * P],
                           src[:, t, 2 * pair:2 * pair + 2, :].rearrange("p h d -> p (h d)"),
                           ident[:])
                m.then_inc(mT_mm, 1)

            pe.wait_ge(wo_in, 32)
            pe.wait_ge(mT_act, 2 * PAIRS)
            pe.wait_ge(mT_dve, 2 * PAIRS)
            pe.wait_ge(mod_up, 1)

            def router(t):
                pe.wait_ge(h2_up, t + 1)
                if t >= 1:
                    pe.wait_ge(h2T_up, t)
                for k in range(K):
                    m = tr(PS[:, 4 + k // 4, (k % 4) * P:(k % 4 + 1) * P],
                           h2[:, t % 2, k * P:(k + 1) * P], ident[:])
                m.then_inc(h2_T, 1)
                pe.wait_ge(h2T_up, t + 1)
                if t >= 1:
                    pe.wait_ge(rt_out, t)
                for k in range(K):
                    m = mm(PS[:, 6, 0:G + E_ALL], h2T[:, t % 2, k, :], rw[:, k, :],
                           start=(k == 0), stop=(k == K - 1))
                m.then_inc(rt_mm, 1)

            for t in range(T):
                if t >= 2:
                    pe.wait_ge(y_gated, t - 1)
                for k in range(K):
                    w = wo_a[:, k, :] if k < 6 else wo_b[:, k - 6, :]
                    for h in range(2):
                        m = mm(PS[:, t % 2 * 2 + h, :], PT[:, k, tokens(t)],
                               w[:, h * CH:(h + 1) * CH], start=(k == 0), stop=(k == K - 1))
                m.then_inc(y_mm, 1)
                if t >= 1:
                    router(t - 1)
            router(T - 1)

            pe.wait_ge(masks_up, 1)
            mm(PS[:, 0, 0:T * E_ALL], before[:], both[:].rearrange("p t e -> p (t e)"),
               start=True, stop=True)
            mm(PS[:, 1, 0:T * E_ALL], ones[:], both[:].rearrange("p t e -> p (t e)"),
               start=True, stop=True).then_inc(rank_mm, 1)

            def turn_x(j, s, first):
                pe.wait_ge(xg_in[s], 16 * (j - s) // 2 + 16 if isinstance(j, int) else 8 * (j - s) + 16)
                if not first:
                    pe.wait_ge(xT_act, j)
                    pe.wait_ge(xT_dve, j)
                for k in range(K):
                    m = tr(PS[:, k // 4, (k % 4) * P:(k % 4 + 1) * P],
                           XG[:, s, k * P:(k + 1) * P], ident[:])
                m.then_inc(xT_mm, 1)

            def expert(i, s, first, last):
                j = 2 * i + s
                pe.wait_ge(gu_in[s], 32 * i + 32)
                pe.wait_ge(xT_act, j + 1)
                pe.wait_ge(xT_dve, j + 1)
                if not first:
                    pe.wait_ge(sil_up, j)
                for k in range(K):
                    m = mm(PS[:, 2, :], XT[:, s, k, :], wg[:, s, k, :],
                           start=(k == 0), stop=(k == K - 1))
                m.then_inc(g_mm, 1)
                if not first:
                    pe.wait_ge(hid_up, j)
                for k in range(K):
                    m = mm(PS[:, 3, :], XT[:, s, k, :], wu[:, s, k, :],
                           start=(k == 0), stop=(k == K - 1))
                m.then_inc(u_mm, 1)
                if not last:
                    turn_x(j + 1, 1 - s, False)
                pe.wait_ge(hid_up, j + 1)
                if not first:
                    pe.wait_ge(hT_up, j)
                for k in range(FC):
                    m = tr(PS[:, 4, k * P:(k + 1) * P], hid[:, k * P:(k + 1) * P], ident[:])
                m.then_inc(hT_mm, 1)
                pe.wait_ge(hT_up, j + 1)
                pe.wait_ge(d_in[s], 16 * i + 16)
                for h, read in enumerate((y_act, y_dve)):
                    if not first:
                        pe.wait_ge(read, j)
                    for k in range(FC):
                        m = mm(PS[:, 5 + h, :], hidT[:, k, :], wd[:, s, k, h * CH:(h + 1) * CH],
                               start=(k == 0), stop=(k == FC - 1))
                    m.then_inc(dn_mm, 1)

            turn_x(0, 0, True)
            expert(0, 0, True, False)
            expert(0, 1, False, False)
            with pe.Fori(1, TILES // 2 - 1) as i:
                for s in range(2):
                    expert(i, s, False, False)
            expert(TILES // 2 - 1, 0, False, False)
            expert(TILES // 2 - 1, 1, False, True)

        @block.scalar
        def _(act):
            A = nc.scalar.activation
            act.dma_start(X[:, 4:8], x_v[:, 4:8]).then_inc(x_in, 16)
            act.dma_start(mod[:].rearrange("p n e -> p (n e)"),
                          a["b_ada"].partition_broadcast(P).rearrange("p a e -> p (a e)"))\
                .then_inc(bada_in, 16)
            for dst, src in ((g1c[:], col(a["norm1_g"])), (foxg[:], col(a["fox_norm_g"])),
                             (hgrng[:], col(a["hgrn_norm_g"])), (lbl[:], col(a["hgrn_lb_logits"])),
                             (pscale[:], col(a["pool_scale"])),
                             (fbias[:], a["fox_f_bias"].partition_broadcast(P).rearrange("p a e -> p (a e)")),
                             (rbias[:, 0:G], a["router_group_b"].partition_broadcast(P).rearrange("p a e -> p (a e)")),
                             (rbias[:, G:], a["router_expert_b"].partition_broadcast(P).rearrange("p a e -> p (a e)")),
                             (rw[:, :, 0:G], a["router_group_w"][0].rearrange("(k p) e -> p k e", p=P)),
                             (rw[:, :, G:], a["router_expert_w"][0].rearrange("(k p) e -> p k e", p=P))):
                act.dma_start(dst, src, allow_slow_non_contiguous=True).then_inc(small_in, 16)
            act.wait_ge(consts, 1)
            for g in range(4):
                r = slice(HD * (g % 2), HD * (g % 2 + 1))
                act.dma_start(pool_w[r, g // 2, r], a["pool_w"][0, g]).then_inc(small_in, 16)
            act.wait_ge(c_in, 16)
            A(c_silu[:], c_raw[:], ACT.Silu).then_inc(silu_c, 1)
            act.wait_ge(x_in, 32)
            for t in range(T):
                if t >= 1:
                    act.wait_ge(x_sq, t)
                A(junk[:], X[:, t, :], ACT.Square, accum_out=ss[:, t:t + 1]).then_inc(x_sq, 1)
            act.wait_ge(cols_up, 2)
            for j in range(0, 2 * K, 2):
                act.wait_ge(tx_done, j + 1)
                k = j // 2
                A(hT[:, k, 0:HALF], PS[:, j % 8, :], ACT.Identity, bias=shift1c[:, k:k + 1],
                  scale=scale1c[:, k:k + 1]).then_inc(ht_act, 1)
            act.wait_ge(consts, 1)
            for t in range(T):
                act.wait_ge(v_mm, t + 1)
                A(VA[:, t, :, 0:HD], PS[:, 2 * t % 8, 0:FOX].rearrange("p (h d) -> p h d", d=HD),
                  ACT.Copy).then_inc(va_out, 1)

            def proj_copy(b):
                act.wait_ge(proj_mm, 2 * b + 1)
                A(PT[:, b, 0:HALF], PS[:, 2 * s, :], ACT.Copy).then_inc(pt_act, 1)

            with act.Fori(0, NB // 3) as i:
                for s in range(3):
                    proj_copy(3 * i + s)
            for s in range(NB % 3):
                proj_copy(NB // 3 * 3 + s)
            act.wait_ge(pt_act, NB)
            act.wait_ge(pt_dve, NB)
            A(PT[:, B_HQ:B_HQ + 3, :], PT[:, B_HQ:B_HQ + 3, :], ACT.Silu).then_inc(silu_up, 1)
            A(PT[:, B_HG:B_HG + 3, :], PT[:, B_HG:B_HG + 3, :], ACT.Silu).then_inc(silu_up, 1)
            A(PT[:, B_HF:B_HF + 3, :], PT[:, B_HF:B_HF + 3, :], ACT.Sigmoid).then_inc(silu_up, 1)
            act.wait_ge(gate_up, 1)
            A(gate_exp[:], gate_abs[:], ACT.Exp, scale=-1.0).then_inc(act_step, 1)
            act.wait_ge(act_step, 1)
            A(gate_ln[:], gate_exp[:], ACT.Ln, bias=1.0).then_inc(gate_ln_up, 1)
            A(lbe[:], lbd[:], ACT.Exp).then_inc(gate_ln_up, 1)

            def fox_pair(i, first):
                for n in range(18):
                    if 1 <= n < 17:
                        m = n - 1
                        act.wait_ge(t_done, 16 * i + m + 1)
                        if not first or m >= 2:
                            act.wait_ge(pv_done, 16 * i + m - 1)
                        w = min(m % 8 + 1, 4)
                        A(probT[:, m % 2, 0:w, :].rearrange("p k q -> p (k q)"),
                          PS[:, 4, 0:w * P], ACT.Copy).then_inc(pta, 1)
                    if n < 16:
                        act.wait_ge(max_up, 16 * i + n + 1)
                        if not first or n >= 2:
                            act.wait_ge(t_done, 16 * i + n - 1)
                        w = (n % 8 + 1) * P
                        src = PS[:, n % 2 * 2:n % 2 * 2 + 2, :].rearrange("p b e -> p (b e)")
                        A(prob[:, n % 2, 0:w], src[:, 0:w], ACT.Exp,
                          bias=nmax[:, n % 2:n % 2 + 1]).then_inc(p_up, 1)
                    if n >= 2:
                        m = n - 2
                        act.wait_ge(pv_done, 16 * i + m + 1)
                        A(OF[:, m % 8, 2 * i + m // 8, :], PS[:, 6 + m % 2, 0:HD + 1],
                          ACT.Copy).then_inc(o_out, 1)

            fox_pair(0, True)
            with act.Fori(1, PAIRS) as i:
                fox_pair(i, False)

            act.wait_ge(pool_mm, 1)
            for b in range(2):
                m = A(PT[:, B_PU + b, :], PS[:, 2 * b:2 * b + 2, :].rearrange("p b e -> p (b e)"),
                      ACT.Copy, scale=pscale[:, b:b + 1])
            m.then_inc(pool_out, 1)

            def hgrn_pair(i, first):
                act.wait_ge(k_up, i + 1)
                A(dec[:, 1, :], dec[:, 0, :], ACT.Ln).then_inc(logf_up, 1)
                act.wait_ge(b_up, i + 1)
                ends = bsum[:].rearrange("p (c t) -> p c t", t=P)[:, :, P - 1]
                A(el[:], ends, ACT.Exp)
                if not first:
                    act.wait_ge(ho_mm, i)
                A(qe[:], bsum[:], ACT.Exp).then_inc(qe_exp, 1)
                act.wait_ge(kd_d, i + 1)
                A(dec[:, 0, :], dec[:, 0, :], ACT.Exp, scale=-1.0).then_inc(kd_e, 1)
                for lv in range(LEVELS):
                    act.wait_ge(d_up, LEVELS * i + lv + 1)
                    half = P >> (lv + 1)
                    v = dec[:, (lv + 1) % 2, :].rearrange("p (n h t) -> p n h t", h=2, t=half)
                    A(v[:, :, 1, :], v[:, :, 1, :], ACT.Exp)
                    A(v[:, :, 0, :], v[:, :, 0, :], ACT.Exp, scale=-1.0).then_inc(e_up, 1)
                    if lv == 0:
                        act.wait_ge(kdT_mm, i + 1)
                        if not first:
                            act.wait_ge(ds_mm, i)
                        A(kdT[:].rearrange("p c t -> p (c t)"),
                          PS[:, 4:6, :].rearrange("p b e -> p (b e)"), ACT.Copy).then_inc(kdT_up, 1)
                act.wait_ge(ho_mm, i + 1)
                A(HO[:, :, bass.ds(2 * i, 2), :],
                  PS[:, 4:6, :].rearrange("p e (c d) -> p c e d", d=HD),
                  ACT.Copy).then_inc(ho_out, 1)

            hgrn_pair(0, True)
            with act.Fori(1, PAIRS) as i:
                hgrn_pair(i, False)
            act.wait_ge(ho_out, PAIRS)
            for g, src in enumerate((ON, HO)):
                act.wait_ge(fsq_in, g + 1)
                A(heads(sq[:]), heads(src[:]), ACT.Square).then_inc(fsq, 1)
            for j in range(0, 4 * PAIRS, 2):
                act.wait_ge(mT_mm, j + 1)
                g, r = j // (2 * PAIRS), j % (2 * PAIRS)
                if g == 0:
                    A(PT[:, r // 2, 0:HALF], PS[:, j % 8, :], ACT.Copy,
                      scale=foxg[:, r // 2:r // 2 + 1]).then_inc(mT_act, 1)
                else:
                    A(PT[:, B_HQ + r // 2, 0:HALF], PS[:, j % 8, :], ACT.Copy,
                      scale=hgrng[:, r // 2:r // 2 + 1]).then_inc(mT_act, 1)
            act.wait_ge(mT_mm, 4 * PAIRS)

            def h2_turned(t):
                act.wait_ge(h2_T, t + 1)
                if t >= 2:
                    act.wait_ge(rt_mm, t - 1)
                A(h2T[:, t % 2].rearrange("p k q -> p (k q)"),
                  PS[:, 4:6, :].rearrange("p b e -> p (b e)"), ACT.Copy).then_inc(h2T_up, 1)

            for t in range(T):
                act.wait_ge(x2_up, t + 1)
                if t >= 1:
                    act.wait_ge(x2_sq, t)
                A(junk2[:], X[:, t, :], ACT.Square, accum_out=ss[:, t:t + 1]).then_inc(x2_sq, 1)
                if t >= 1:
                    h2_turned(t - 1)
            h2_turned(T - 1)
            act.wait_ge(r_exp_in, 1)
            A(gexp[:], gdif[:], ACT.Exp).then_inc(r_exp, 1)
            act.wait_ge(r_exp_in, 2)
            A(lexp[:], ldif[:], ACT.Exp).then_inc(r_exp, 1)

            def x_turned(j, s, first):
                act.wait_ge(xT_mm, j + 1)
                if not first:
                    act.wait_ge(u_mm, j - 1)
                A(XT[:, s, 0:4, :].rearrange("p k q -> p (k q)"), PS[:, 0, :],
                  ACT.Copy).then_inc(xT_act, 1)

            def expert(i, s, first, last):
                j = 2 * i + s
                act.wait_ge(g_mm, j + 1)
                if not first:
                    act.wait_ge(hid_up, j)
                A(sil[:], PS[:, 2, :], ACT.Silu).then_inc(sil_up, 1)
                if not last:
                    x_turned(j + 1, 1 - s, first)
                act.wait_ge(hT_mm, j + 1)
                if not first:
                    act.wait_ge(dn_mm, 2 * j)
                A(hidT[:].rearrange("p k q -> p (k q)"), PS[:, 4, :], ACT.Copy).then_inc(hT_up, 1)
                act.wait_ge(dn_mm, 2 * j + 1)
                if not isinstance(i, int) or i >= 1:
                    act.wait_ge(y_out[s], 16 * i)
                A(Y[:, s, 0:CH], PS[:, 5, :], ACT.Copy).then_inc(y_act, 1)
                act.wait_ge(y_act, j + 1)
                act.wait_ge(y_dve, j + 1)
                act.dma_start(y_rows[bass.ds(P * j, P), :], Y[:, s, :]).then_inc(y_out[s], 16)

            x_turned(0, 0, True)
            expert(0, 0, True, False)
            expert(0, 1, False, False)
            with act.Fori(1, TILES // 2 - 1) as i:
                for s in range(2):
                    expert(i, s, False, False)
            expert(TILES // 2 - 1, 0, False, False)
            expert(TILES // 2 - 1, 1, False, True)
            act.wait_ge(dn_mm, 2 * TILES)
            act.dma_start(gf[:], a["final_norm_g"].partition_broadcast(P)).then_inc(gf_in, 16)
            for t in range(T):
                act.wait_ge(x3_up, t + 1)
                if t >= 1:
                    act.wait_ge(x3_sq, t)
                A(junk3[:], X[:, t, :], ACT.Square, accum_out=ss[:, t:t + 1]).then_inc(x3_sq, 1)

        @block.vector
        def _(v):
            V = nc.vector
            step = Chain(v, dve_step)
            v.wait_ge(silu_c, 1)
            V.tensor_copy(c_wide[:], c_silu[:].unsqueeze(2).broadcast_to([P, K, P]))\
                .then_inc(c_wide_up, 1)
            v.wait_ge(bada_in, 16)
            with v.Fori(0, MOD_N) as i:
                for s in range(2):
                    v.wait_ge(ada_mm, 2 * i + s + 1)
                    V.tensor_tensor(mod[:, 2 * i + s, :], PS[:, s, :], mod[:, 2 * i + s, :],
                                    ALU.add).then_inc(ada_out, 1)
            v.wait_ge(small_in, 16 * N_SMALL)
            v.wait_ge(cols_mm, 1)
            V.scalar_tensor_tensor(scale1c[:], PS[:, 2, K:2 * K], 1.0, g1c[:], ALU.add,
                                   ALU.mult).then_inc(cols_up, 1)
            V.tensor_copy(shift1c[:], PS[:, 2, 0:K]).then_inc(cols_up, 1)
            v.wait_ge(cols_up, 2)
            for j in range(1, 2 * K, 2):
                v.wait_ge(tx_done, j + 1)
                k = j // 2
                V.tensor_scalar(hT[:, k, HALF:S], PS[:, j % 8, :], scale1c[:, k:k + 1],
                                shift1c[:, k:k + 1], ALU.mult, ALU.add).then_inc(ht_dve, 1)
            v.wait_ge(ada_out, 2 * MOD_N)
            for n in (4, 8, 10):
                step(V.tensor_scalar(mod[:, n:n + 2, :], mod[:, n:n + 2, :], 1.0, None, ALU.add))
            step(V.tensor_tensor(lbd[:], lbl[:], lbl[:], ALU.subtract))
            for t in range(T):
                v.wait_ge(v_mm, t + 1)
                v.wait_ge(va_out, t + 1)
                b = 2 * t % 8
                V.tensor_tensor(gate[:, t, :], PS[:, b, FOX:VW], fbias[:], ALU.add)
                V.tensor_copy(HI[:, t, :], PS[:, b + 1, 0:HG]).then_inc(hi_out, 1)
            v.wait_ge(hi_out, T)
            V.scalar_tensor_tensor(gate_abs[:], gate[:], -1.0, gate[:], ALU.mult, ALU.max)\
                .then_inc(gate_up, 1)

            def proj_copy(b, s):
                v.wait_ge(proj_mm, 2 * b + 2)
                V.tensor_copy(PT[:, b, HALF:S], PS[:, 2 * s + 1, :]).then_inc(pt_dve, 1)

            with v.Fori(0, NB // 3) as i:
                for s in range(3):
                    proj_copy(3 * i + s, s)
            for s in range(NB % 3):
                proj_copy(NB // 3 * 3 + s, s)
            v.wait_ge(gate_ln_up, 2)
            V.scalar_tensor_tensor(log_forget[:], gate[:], 0.0, gate_ln[:], ALU.min,
                                   ALU.subtract).then_inc(lf_up, 1)
            step(V.memset(ones_row[:], 1.0))
            v.wait_ge(lf_T, 1)
            V.tensor_tensor_scan(f_sum[:], ones_row[:],
                                 PS[0:NH, 6:8, :].rearrange("p b e -> p (b e)"), 0.0, ALU.mult,
                                 ALU.add).then_inc(f_up, 1)
            v.wait_ge(f_up, 1)
            V.tensor_scalar(f_neg[:], f_sum[:], -1.0, None, ALU.mult).then_inc(f_up, 1)
            step(V.reciprocal(lbr[:], lbe[:]))
            step(V.tensor_tensor(lbp[:], lbe[:], lbr[:], ALU.mult))
            step(V.tensor_tensor(lb[:], lbp[:], lbp[:], ALU.subtract))
            step(V.tensor_scalar(oml[:], lb[:], -1.0, 1.0, ALU.mult, ALU.add))

            def fox_pair(i, first):
                step.enter(i, 16)
                for n in range(17):
                    if n < 16:
                        q = n % 8
                        v.wait_ge(s_done, 16 * i + n + 1)
                        dg = PS[:, n % 2 * 2 + q // 4, q % 4 * P:(q % 4 + 1) * P]
                        step(V.tensor_tensor(dg, dg, causal[:], ALU.add))
                        src = PS[:, n % 2 * 2:n % 2 * 2 + 2, :].rearrange("p b e -> p (b e)")
                        V.tensor_reduce(nmax[:, n % 2:n % 2 + 1], src[:, 0:(q + 1) * P], AX.X,
                                        ALU.max, negate=True).then_inc(max_up, 1)
                    m = n - 1
                    if n >= 1 and m % 8 >= 4:
                        v.wait_ge(t_done, 16 * i + m + 1)
                        v.wait_ge(pv_done, 16 * i + m - 1)
                        w = m % 8 - 3
                        V.tensor_copy(probT[:, m % 2, 4:4 + w, :].rearrange("p k q -> p (k q)"),
                                      PS[:, 5, 0:w * P]).then_inc(ptb, 1)

            v.wait_ge(consts, 1)
            v.wait_ge(rows_out, 32)
            fox_pair(0, True)
            step.leave(1)
            keep = step.n
            step.n = keep - 16
            with v.Fori(1, PAIRS) as i:
                fox_pair(i, False)
            step.leave(PAIRS)

            v.wait_ge(silu_up, 3)
            v.wait_ge(s_done, 16 * PAIRS)
            v.wait_ge(pv_done, 16 * PAIRS)
            v.wait_ge(pool_out, 1)
            v.wait_ge(qk_in[0], 64 * PAIRS)
            v.wait_ge(qk_in[1], 64 * PAIRS)
            step(V.memset(scores[:].rearrange("p e c t -> p (e c t)"), 0.0))
            step(V.memset(carry[:], 1.0))
            step(V.memset(carry[:].rearrange("p (c t) -> p c t", t=P)[:, :, 0:1], 0.0))
            bc = bsum[:].rearrange("p (c t) -> p c t", t=P)

            def level(i, lv, first):
                half = P >> (lv + 1)
                b = bsum[:].rearrange("p (n h t) -> p n h t", h=2, t=half)
                d = dec[:, (lv + 1) % 2, :].rearrange("p (n h t) -> p n h t", h=2, t=half)
                m = b[:, :, 0, half - 1:half].unsqueeze(2).broadcast_to([P, S // (2 * half), 2, half])
                if lv == 1:
                    v.wait_ge(kdT_mm, i + 1)
                if lv >= 2:
                    v.wait_ge(g_up, LEVELS * i + lv - 1)
                V.tensor_tensor(d, b, m, ALU.subtract).then_inc(d_up, 1)

            def merge_level(i, lv, mask):
                for st in range(2):
                    v.wait_ge(lv_mm, 16 * i + 2 * lv + st + 1)
                    V.memset(waited[:, 2 * lv + st:2 * lv + st + 1], 0.0)
                    for e in range(2):
                        m = V.copy_predicated(
                            scores[:, e, 4 * st:4 * st + 4, :],
                            mask.bitcast(U32).unsqueeze(1).broadcast_to([P, 4, P]),
                            PS[:, 2 * st + e, :].rearrange("p (c t) -> p c t", t=P))
                    m.then_inc(sc_out, 1)

            def hgrn_pair(i, first):
                step.enter(i, 9)
                if not first:
                    v.wait_ge(g_up, LEVELS * i)
                    v.wait_ge(ho_mm, i)
                step(V.tensor_scalar(dec[:, 0, :], PT[:, B_HF + i, :], oml[:, bass.ds(i, 1)],
                                     lb[:, bass.ds(i, 1)], ALU.mult, ALU.add))
                step(V.tensor_scalar(dec[:, 0, :], dec[:, 0, :], 1e-19, None, ALU.max))
                V.tensor_scalar(kb[:], dec[:, 0, :], -1.0, 1.0, ALU.mult, ALU.add)\
                    .then_inc(k_up, 1)
                v.wait_ge(logf_up, i + 1)
                V.tensor_tensor_scan(bsum[:], carry[:], dec[:, 1, :], 0.0, ALU.mult, ALU.add)\
                    .then_inc(b_up, 1)
                v.wait_ge(b_up, i + 1)
                V.tensor_tensor(dec[:, 0, :].rearrange("p (c t) -> p c t", t=P), bc,
                                bc[:, :, P - 1:P].broadcast_to([P, T, P]),
                                ALU.subtract).then_inc(kd_d, 1)
                level(i, 0, first)
                merge_level(i, 0, ident[:])
                for lv in range(LEVELS):
                    if lv + 1 < LEVELS:
                        level(i, lv + 1, first)
                    merge_level(i, lv + 1, level_mask[:, lv, :])
                    if lv == 0:
                        v.wait_ge(ds_mm, i + 1)
                        v.wait_ge(qe_exp, i + 1)
                        for c in range(1, T):
                            for e in range(2):
                                half = slice(HD * e, HD * (e + 1))
                                o = (c - 1) % 4 * P + HD * e
                                ds = PS[half, 6 + (c - 1) // 4, o:o + HD]
                                if c == 1:
                                    m = V.tensor_copy(states[half, c, :], ds)
                                else:
                                    m = V.scalar_tensor_tensor(
                                        states[half, c, :], states[half, c - 1, :],
                                        el[half, c - 1:c], ds, ALU.mult, ALU.add)
                            if c < T - 1:
                                step(m)
                        m.then_inc(st_up, 1)
                step(V.memset(rl[:, 0:1], 0.0))

            hgrn_pair(0, True)
            step.leave(1)
            step.n -= 9
            with v.Fori(1, PAIRS) as i:
                hgrn_pair(i, False)
            step.leave(PAIRS)
            v.wait_ge(ho_mm, PAIRS)
            v.wait_ge(o_out, 16 * PAIRS)
            of = heads(OF[:])
            step(V.reciprocal(rl[:], of[:, :, HD]))
            V.tensor_tensor(heads(ON[:]), of[:, :, 0:HD],
                            rl[:].unsqueeze(2).broadcast_to([P, T * NH, HD]),
                            ALU.mult).then_inc(fsq_in, 1)
            for g, src in enumerate((ON, HO)):
                v.wait_ge(fsq, g + 1)
                V.tensor_reduce(head_ss[:, g, :], heads(sq[:]), AX.X, ALU.add).then_inc(fss, 1)
                if g == 0:
                    v.wait_ge(ho_out, PAIRS)
                    v.wait_ge(fss, 1)
                    V.memset(rl[:, 0:1], 0.0).then_inc(fsq_in, 1)
                v.wait_ge(frs, g + 1)
                V.tensor_tensor(heads(src[:]), heads(src[:]),
                                head_r[:, g, :].unsqueeze(2).broadcast_to([P, T * NH, HD]),
                                ALU.mult).then_inc(on_up, 1)
            for j in range(1, 4 * PAIRS, 2):
                v.wait_ge(mT_mm, j + 1)
                g, r = j // (2 * PAIRS), j % (2 * PAIRS)
                gain, blk = ((foxg, 0), (hgrng, B_HQ))[g]
                V.tensor_scalar(PT[:, blk + r // 2, HALF:S], PS[:, j % 8, :],
                                gain[:, r // 2:r // 2 + 1], None, ALU.mult).then_inc(mT_dve, 1)
            v.wait_ge(mT_act, 2 * PAIRS)
            v.wait_ge(mT_dve, 2 * PAIRS)
            V.tensor_tensor(PT[:, B_HQ:B_HQ + 3, :], PT[:, B_HQ:B_HQ + 3, :],
                            PT[:, B_HG:B_HG + 3, :], ALU.mult).then_inc(mod_up, 1)
            v.wait_ge(g2_in, 16)
            m8 = mod[:, 8:10, :].rearrange("p n e -> p (n e)")
            V.tensor_tensor(m8, m8, g2[:], ALU.mult).then_inc(mod_up, 1)
            v.wait_ge(mod_up, 2)

            def second_norm(t):
                v.wait_ge(h2_r, t + 1)
                if t >= 2:
                    v.wait_ge(h2_out[t % 2], 16 * (t // 2))
                    v.wait_ge(h2_T, t - 1)
                V.scalar_tensor_tensor(h2[:, t % 2, :], X[:, t, :], rstd[:, t:t + 1], m8,
                                       ALU.mult, ALU.mult).then_inc(h2_m, 1)

            for t in range(T):
                v.wait_ge(y_mm, t + 1)
                if t >= 2:
                    v.wait_ge(x2_up, t - 1)
                V.tensor_tensor(ytmp[:, t % 2, :],
                                PS[:, t % 2 * 2:t % 2 * 2 + 2, :].rearrange("p b e -> p (b e)"),
                                mod[:, 4:6, :].rearrange("p n e -> p (n e)"),
                                ALU.mult).then_inc(y_gated, 1)
                second_norm(t)
                if t >= 1:
                    v.wait_ge(rt_mm, t)
                    V.tensor_tensor(logits[:, t - 1, :], PS[:, 6, 0:G + E_ALL], rbias[:],
                                    ALU.add).then_inc(rt_out, 1)
            v.wait_ge(rt_mm, T)
            V.tensor_tensor(logits[:, T - 1, :], PS[:, 6, 0:G + E_ALL], rbias[:],
                            ALU.add).then_inc(rt_out, 1)

            v.wait_ge(rt_out, T)
            v.wait_ge(iota_up, 1)
            v.wait_ge(h2T_up, T)
            v.wait_ge(x2_sq, T)

            def wide(ap, n):
                return ap.unsqueeze(2).broadcast_to([P, T, n])

            def first_best(oh, val, best):
                step(V.tensor_tensor(eqv[:], val, wide(best[:], 4), ALU.is_equal))
                step(V.tensor_tensor(eqv[:], eqv[:], first4[:].unsqueeze(1).broadcast_to([P, T, 4]),
                                     ALU.mult))
                step(V.tensor_reduce(fst[:], eqv[:], AX.X, ALU.max))
                step(V.tensor_tensor(oh[:], first4[:].unsqueeze(1).broadcast_to([P, T, 4]),
                                     wide(fst[:], 4), ALU.is_equal))

            gl, xl = logits[:, :, 0:G], logits[:, :, G:]
            step(V.tensor_reduce(gmax[:], gl, AX.X, ALU.max))
            V.tensor_tensor(gdif[:], gl, wide(gmax[:], G), ALU.subtract).then_inc(r_exp_in, 1)
            first_best(oh_g, gl, gmax)
            for g in range(G):
                m = V.tensor_tensor(picked[:, :, :, g], xl[:, :, g * EG:(g + 1) * EG],
                                    oh_g[:, :, g:g + 1].broadcast_to([P, T, EG]), ALU.mult)
            step(m)
            step(V.tensor_reduce(local[:], picked[:], AX.X, ALU.add))
            step(V.tensor_reduce(lmax[:], local[:], AX.X, ALU.max))
            first_best(oh_1, local[:], lmax)
            step(V.scalar_tensor_tensor(local2[:], oh_1[:], -1e30, local[:], ALU.mult, ALU.add))
            step(V.tensor_reduce(lmax2[:], local2[:], AX.X, ALU.max))
            first_best(oh_2, local2[:], lmax2)
            V.tensor_tensor(ldif[:], lmax2[:], lmax[:], ALU.subtract).then_inc(r_exp_in, 1)
            for mk, oh in ((m1, oh_1), (m2, oh_2)):
                for g in range(G):
                    m = V.tensor_tensor(mk[:, :, g, :], oh[:],
                                        oh_g[:, :, g:g + 1].broadcast_to([P, T, EG]), ALU.mult)
            step(m)
            flat = lambda ap: ap.rearrange("p t g e -> p t (g e)")
            V.tensor_tensor(both[:], flat(m1[:]), flat(m2[:]), ALU.add).then_inc(masks_up, 1)
            v.wait_ge(r_exp, 2)
            step(V.tensor_reduce(gsum[:], gexp[:], AX.X, ALU.add))
            step(V.reciprocal(pgroup[:], gsum[:]))
            step(V.tensor_scalar(lden[:], lexp[:], 1.0, None, ALU.add))
            step(V.reciprocal(lrec[:], lden[:]))
            step(V.tensor_tensor(w12[:, 0, :], pgroup[:], lrec[:], ALU.mult))
            step(V.tensor_tensor(w12[:, 1, :], w12[:, 0, :], lexp[:], ALU.mult))
            v.wait_ge(rank_mm, 1)
            te = lambda ap: ap.rearrange("p (t e) -> p t e", e=E_ALL)
            step(V.tensor_copy(tot[:], te(PS[:, 1, 0:T * E_ALL])))
            step(V.memset(run[:, 0, :], 0.0))
            for t in range(T):
                step(V.tensor_tensor(run[:, t + 1, :], run[:, t, :], tot[:, t, :], ALU.add))
            step(V.tensor_tensor(rank[:], te(PS[:, 0, 0:T * E_ALL]), run[:, 0:T, :], ALU.add))
            step(V.tensor_tensor(hund[:], run[:, T, :].unsqueeze(2).broadcast_to([P, E_ALL, T]),
                                 step128[:].unsqueeze(1).broadcast_to([P, E_ALL, T]), ALU.is_gt))
            step(V.tensor_reduce(ntile[:], hund[:], AX.X, ALU.add))
            step(V.tensor_tensor_scan(tend[:], ones[:, 0:E_ALL], ntile[:], 0.0, ALU.mult, ALU.add))
            step(V.tensor_tensor(tbase[:], tend[:], ntile[:], ALU.subtract))
            step(V.scalar_tensor_tensor(pos[:], tbase[:].unsqueeze(1).broadcast_to([P, T, E_ALL]),
                                        float(P), rank[:], ALU.mult, ALU.add))
            for n, mk in enumerate((m1, m2)):
                step(V.tensor_tensor(pick[:], pos[:], flat(mk[:]), ALU.mult))
                step(V.tensor_reduce(slots[:, n, :], pick[:], AX.X, ALU.add))
            step(V.tensor_copy(slots_i[:], slots[:]))
            step(V.tensor_tensor(t_cmp[:], tend[:].unsqueeze(1).broadcast_to([P, TILES, E_ALL]),
                                 tile_no[:].unsqueeze(2).broadcast_to([P, TILES, E_ALL]),
                                 ALU.is_le))
            step(V.tensor_reduce(t_exp[:], t_cmp[:], AX.X, ALU.add))
            step(V.tensor_scalar(t_exp[:], t_exp[:], float(E_ALL - 1), None, ALU.min))
            V.tensor_copy(t_exp_i[:], t_exp[:]).then_inc(slots_up, 1)

            def x_turned(j, s, first):
                v.wait_ge(xT_mm, j + 1)
                if not first:
                    v.wait_ge(u_mm, j - 1)
                V.tensor_copy(XT[:, s, 4:8, :].rearrange("p k q -> p (k q)"),
                              PS[:, 1, :]).then_inc(xT_dve, 1)

            def expert(i, s, first, last):
                j = 2 * i + s
                v.wait_ge(u_mm, j + 1)
                v.wait_ge(sil_up, j + 1)
                if not first:
                    v.wait_ge(hT_mm, j)
                V.tensor_tensor(hid[:], PS[:, 3, :], sil[:], ALU.mult).then_inc(hid_up, 1)
                if not last:
                    x_turned(j + 1, 1 - s, first)
                v.wait_ge(dn_mm, 2 * j + 2)
                if not isinstance(i, int) or i >= 1:
                    v.wait_ge(y_out[s], 16 * i)
                V.tensor_copy(Y[:, s, CH:D], PS[:, 6, :]).then_inc(y_dve, 1)

            v.wait_ge(zeros_out, 16)
            v.wait_ge(slots_out, 32 * T)
            x_turned(0, 0, True)
            expert(0, 0, True, False)
            expert(0, 1, False, False)
            with v.Fori(1, TILES // 2 - 1) as i:
                for s in range(2):
                    expert(i, s, False, False)
            expert(TILES // 2 - 1, 0, False, False)
            expert(TILES // 2 - 1, 1, False, True)
            v.wait_ge(gf_in, 16)
            g2v = mod[:, 10:12, :].rearrange("p n e -> p (n e)")
            for t in range(T):
                s = t % 2
                v.wait_ge(ya_in[s], 16 * (t // 2 + 1))
                v.wait_ge(yb_in[s], 16 * (t // 2 + 1))
                step(V.tensor_scalar(ya[:, s, :], ya[:, s, :], w12[:, 0, t:t + 1], None, ALU.mult))
                step(V.scalar_tensor_tensor(ya[:, s, :], yb[:, s, :], w12[:, 1, t:t + 1],
                                            ya[:, s, :], ALU.mult, ALU.add))
                step(V.tensor_tensor(ya[:, s, :], ya[:, s, :], g2v, ALU.mult))
                V.tensor_tensor(X[:, t, :], X[:, t, :], ya[:, s, :], ALU.add).then_inc(x3_up, 1)
                v.wait_ge(x3_r, t + 1)
                if t >= 2:
                    v.wait_ge(fin_out[s], 16 * (t // 2))
                V.scalar_tensor_tensor(fin[:, s, :], X[:, t, :], rstd[:, t:t + 1], gf[:], ALU.mult,
                                       ALU.mult).then_inc(fin_up, 1)

        @block.gpsimd
        def _(pool):
            G_ = nc.gpsimd
            step = Chain(pool, pool_step)

            def select(ap, pattern, base, cm, op=ALU.is_ge, fill=0.0):
                return G_.affine_select(out=ap, in_=ap, pattern=pattern, compare_op=op, fill=fill,
                                        base=base, channel_multiplier=cm)

            G_.memset(ones[:], 1.0)
            G_.memset(causal[:], 0.0)
            G_.memset(level_mask[:].rearrange("p l t -> p (l t)"), 0.0)
            G_.memset(pool_w[:].rearrange("p l t -> p (l t)"), 0.0)
            G_.memset(power[:], -0.5)
            G_.memset(before[:], 1.0)
            step(G_.memset(ident[:], 0.0))
            select(ident[:], [[-1, P]], 0, 1, ALU.not_equal, 1.0)
            select(before[:], [[1, P]], -1, -1)
            step(select(causal[:], [[-1, P]], 0, 1, fill=-1e30))
            for lv in range(LEVELS):
                half = P >> (lv + 1)
                m = level_mask[:, lv, :].rearrange("p (n h t) -> p n h t", h=2, t=half)[:, :, 1, :]
                n = P // (2 * half)
                step(G_.memset(m, 1.0))
                step(select(m, [[-2 * half, n], [0, half]], 0, 1))
                step(select(m, [[2 * half, n], [0, half]], half - 1, -1))
            for b in range(2):
                for h in range(2):
                    w = 2 << (2 * b + h)
                    r = slice(HD * h, HD * (h + 1))
                    step(G_.memset(wcol[r, b:b + 1], float(w)))
                    step(G_.memset(iwcol[r, b:b + 1], 1.0 / w))
                    step(G_.iota(invc[r, b, :], [[1, 16]], base=1, channel_multiplier=0,
                                allow_small_or_imprecise_dtypes=True))
            for b in range(2):
                m = G_.tensor_scalar(invc[:, b, :], invc[:, b, :], wcol[:, b:b + 1], None, ALU.min)
            step(m)
            G_.memset(VA[:, :, :, HD:HD + 1].rearrange("p t h d -> p (t h) d"), 1.0)\
                .then_inc(consts, 1)
            for t in range(T):
                pool.wait_ge(x_sq, t + 1)
                step(G_.tensor_scalar(ms[:, t:t + 1], ss[:, t:t + 1], 1.0 / D, EPS, ALU.mult,
                                      ALU.add))
                step(G_.tensor_tensor(rstd[:, t:t + 1], ms[:, t:t + 1], power[:, 0:1], ALU.pow))
                G_.tensor_scalar(xhat[:, t, :], X[:, t, :], rstd[:, t:t + 1], None, ALU.mult)\
                    .then_inc(x_hat, 1)
            pool.wait_ge(pt_act, NB)
            pool.wait_ge(pt_dve, NB)
            for j in range(3):
                G_.tensor_scalar(PT[:, B_FQ + j, :], PT[:, B_FQ + j, :], float(HD) ** -0.5, None,
                                 ALU.mult).then_inc(q_scaled, 1)
            pool.wait_ge(q_scaled, 3)
            for e in range(2):
                step(G_.memset(QA[e][HD:HD + 2, :], 1.0))
                step(G_.memset(KA[e][HD:HD + 2, :], 1.0))
            G_.memset(head_ms[:, 0, 0:32], -1.0).then_inc(q_scaled, 1)
            pool.wait_ge(q_scaled, 4)
            for b in range(2):
                step(G_.tensor_tensor(invc[:, b, :], invc[:, b, :], head_ms[:, 0, 0:16], ALU.pow))
            for b in range(2):
                u = PT[:, B_PU + b, :]
                src, width, dst = u, 1, 0
                for d in range(2 * b + 2):
                    if d == 2 * b + 1:
                        rows = slice(HD, P)
                    else:
                        rows = slice(0, P)
                    o = win_sum[rows, dst, :]
                    step(G_.tensor_copy(o[:, 0:width], src[rows, 0:width]))
                    step(G_.tensor_tensor(o[:, width:S], src[rows, width:S],
                                          src[rows, 0:S - width], ALU.add))
                    if rows == slice(HD, P):
                        last = dst
                    src, width, dst = win_sum[:, dst, :], 2 * width, 1 - dst
                for h, buf in ((0, 1 - last), (1, last)):
                    r = slice(HD * h, HD * (h + 1))
                    w = win_sum[r, buf, :]
                    step(G_.tensor_tensor(w[:, 0:16], w[:, 0:16], invc[r, b, :], ALU.mult))
                    step(G_.tensor_scalar(w[:, 16:S], w[:, 16:S], iwcol[r, b:b + 1], None, ALU.mult))
                    step(G_.tensor_tensor(PT[r, B_PU + b, :], w, PT[r, B_PU + b, :], ALU.subtract))
                G_.memset(head_ms[:, 0, 32:33], 0.0).then_inc(pooled_up, 1)

            def hgrn_pair(i, first):
                if first:
                    pool.wait_ge(silu_up, 3)
                    pool.wait_ge(s_done, 16 * PAIRS)
                    pool.wait_ge(pool_out, 1)
                else:
                    pool.wait_ge(lv_mm, 16 * i)
                G_.tensor_copy(qb[:], PT[:, B_HQ + i, :]).then_inc(q_up, 1)
                pool.wait_ge(q_up, i + 1)
                pool.wait_ge(kd_e, i + 1)
                G_.tensor_tensor(dec[:, 0, :], dec[:, 0, :], kb[:], ALU.mult).then_inc(kd_up, 1)
                for lv in range(LEVELS):
                    pool.wait_ge(e_up, LEVELS * i + lv + 1)
                    if not first or lv >= 2:
                        pool.wait_ge(lv_mm, 16 * i + 2 * lv - 2)
                    half = P >> (lv + 1)
                    cut = lambda ap: ap.rearrange("p (n h t) -> p n h t", h=2, t=half)
                    d, g = cut(dec[:, (lv + 1) % 2, :]), cut(gk[:, lv % 2, :])
                    G_.tensor_tensor(g[:, :, 1, :], d[:, :, 1, :], cut(qb[:])[:, :, 1, :], ALU.mult)
                    G_.tensor_tensor(g[:, :, 0, :], d[:, :, 0, :], cut(kb[:])[:, :, 0, :],
                                     ALU.mult).then_inc(g_up, 1)
                    if lv == 0:
                        pool.wait_ge(qe_exp, i + 1)
                        G_.tensor_tensor(qe[:], qe[:], qb[:], ALU.mult).then_inc(qe_up, 1)

            hgrn_pair(0, True)
            with pool.Fori(1, PAIRS) as i:
                hgrn_pair(i, False)
            for g in range(2):
                pool.wait_ge(fss, g + 1)
                step(G_.tensor_scalar(head_ms[:, g, :], head_ss[:, g, :], 1.0 / HD, EPS, ALU.mult,
                                      ALU.add))
                G_.tensor_tensor(head_r[:, g, :], head_ms[:, g, :], power[:, 0:T * NH],
                                 ALU.pow).then_inc(frs, 1)
            pool.wait_ge(ho_mm, PAIRS)
            pool.wait_ge(on_up, 1)
            pool.dma_start(g2[:], a["norm2_g"].partition_broadcast(P).rearrange("p a e -> p (a e)"))\
                .then_inc(g2_in, 16)

            for t in range(T):
                pool.wait_ge(y_gated, t + 1)
                G_.tensor_tensor(X[:, t, :], X[:, t, :], ytmp[:, t % 2, :], ALU.add)\
                    .then_inc(x2_up, 1)
                pool.wait_ge(x2_sq, t + 1)
                step(G_.tensor_scalar(ms[:, t:t + 1], ss[:, t:t + 1], 1.0 / D, EPS, ALU.mult,
                                      ALU.add))
                G_.tensor_tensor(rstd[:, t:t + 1], ms[:, t:t + 1], power[:, 0:1],
                                 ALU.pow).then_inc(h2_r, 1)
                pool.wait_ge(h2_m, t + 1)
                G_.tensor_tensor(h2[:, t % 2, :], h2[:, t % 2, :],
                                 mod[:, 6:8, :].rearrange("p n e -> p (n e)"),
                                 ALU.add).then_inc(h2_up, 1)
            pool.wait_ge(h2_T, T)
            pool.wait_ge(rt_mm, T)
            pool.wait_ge(y_gated, T)
            for s in range(2):
                pool.wait_ge(h2_out[s], 16 * T // 2)
            G_.iota(token_id[:].bitcast(I32), [[P, T]], base=0, channel_multiplier=1)
            G_.iota(tile_no[:], [[1, TILES]], base=0, channel_multiplier=0,
                    allow_small_or_imprecise_dtypes=True)
            G_.iota(step128[:], [[P, T]], base=0, channel_multiplier=0,
                    allow_small_or_imprecise_dtypes=True)
            G_.iota(first4[:], [[-1, 4]], base=4, channel_multiplier=0,
                    allow_small_or_imprecise_dtypes=True)
            G_.iota(zero_slots[:].bitcast(I32), [[0, TILES]], base=0, channel_multiplier=0)\
                .then_inc(iota_up, 1)
            pool.wait_ge(iota_up, 1)
            pool.dma_start(slot_token.rearrange("(p n) a -> p (n a)", p=P), zero_slots[:])\
                .then_inc(zeros_out, 16)
            pool.wait_ge(zeros_out, 16)
            pool.wait_ge(slots_up, 1)
            for n in range(2):
                for t in range(T):
                    pool.indirect_dma_start(
                        out=slot_token, out_offset=bass.IndirectOffsetOnAxis(
                            ap=slots_i[:, n, t:t + 1], axis=0),
                        in_=token_id[:, t:t + 1], in_offset=None).then_inc(slots_out, 16)
            pool.wait_ge(slots_out, 32 * T)

            def gather(i, s, first):
                j = 2 * i + s
                if not first:
                    pool.wait_ge(xT_mm, j - 1)
                pool.dma_start(tok[:, s:s + 1], slot_token[bass.ds(P * j, P), :])\
                    .then_inc(tok_in[s], 16)
                if not first:
                    pool.wait_ge(tok_seen, j - 1)
                pool.wait_ge(tok_in[s], 16 * i + 16)
                G_.tensor_tensor(waited_pool[:, s:s + 1], power[:, 0:1], power[:, 1:2],
                                 ALU.mult).then_inc(tok_seen, 1)
                pool.indirect_dma_start(
                    out=XG[:, s, :], out_offset=None, in_=h2_rows,
                    in_offset=bass.IndirectOffsetOnAxis(ap=tok[:, s:s + 1], axis=0))\
                    .then_inc(xg_in[s], 16)

            for s in range(2):
                gather(0, s, True)
            with pool.Fori(1, TILES // 2) as i:
                for s in range(2):
                    gather(i, s, False)
            pool.wait_ge(dn_mm, 2 * TILES)
            for s in range(2):
                pool.wait_ge(y_out[s], 16 * TILES // 2)

            def rows_back(t):
                for buf, n, got in ((ya, 0, ya_in), (yb, 1, yb_in)):
                    pool.indirect_dma_start(
                        out=buf[:, t % 2, :], out_offset=None, in_=y_rows,
                        in_offset=bass.IndirectOffsetOnAxis(ap=slots_i[:, n, t:t + 1], axis=0))\
                        .then_inc(got[t % 2], 16)

            for t in range(2):
                rows_back(t)
            for t in range(T):
                pool.wait_ge(x3_sq, t + 1)
                step(G_.tensor_scalar(ms[:, t:t + 1], ss[:, t:t + 1], 1.0 / D, EPS, ALU.mult,
                                      ALU.add))
                G_.tensor_tensor(rstd[:, t:t + 1], ms[:, t:t + 1], power[:, 0:1],
                                 ALU.pow).then_inc(x3_r, 1)
                if t + 2 < T:
                    rows_back(t + 2)


_INS = ['x', 'c', 'w_ada', 'b_ada', 'norm1_g', 'w_in', 'fox_f_bias', 'fox_norm_g', 'hgrn_lb_logits',
        'hgrn_norm_g', 'pool_w', 'pool_scale', 'w_out', 'norm2_g', 'router_group_w',
        'router_group_b', 'router_expert_w', 'router_expert_b', 'expert_w_gate', 'expert_w_up',
        'expert_w_down', 'final_norm_g']


def kernel(**inputs):
    import numpy as _np
    import concourse.bacc as _bacc
    from concourse.bass_utils import run_bass_kernel_spmd as _run

    nc = _bacc.Bacc("TRN2", target_bir_lowering=False, num_devices=1)
    arrays, aps = {}, {}
    for name in _INS:
        v = _np.ascontiguousarray(inputs[name])
        arrays[f"in_{name}"] = v
        aps[name] = nc.dram_tensor(f"in_{name}", v.shape, mybir.dt.from_np(v.dtype),
                                   kind="ExternalInput").ap()
    out = nc.dram_tensor("out", (1, S, D), F32, kind="ExternalOutput").ap()
    build(nc, aps, out)
    r = _run(nc, [arrays], core_ids=[0])
    return r.results[0]["out"]
```

```python
from contextlib import ExitStack

import concourse.bass as bass
from concourse import mybir

F32 = mybir.dt.float32
F32R = mybir.dt.float32r
I32 = mybir.dt.int32
U32 = mybir.dt.uint32
ALU = mybir.AluOpType
ACT = mybir.ActivationFunctionType
AX = mybir.AxisListType

P = 128
D = 1024
S = 1024
K = D // P
T = S // P
HD = 64
FOX = 384
HG = 384
PL = 256
NH = FOX // HD
PAIRS = NH // 2
MOD_N = 6
CH = 512
E_ALL = 16
G = 4
EG = 4
FF = 512
FC = FF // P
EPS = 1e-6
TILES = (2 * S + E_ALL * (P - 1)) // P
WIDE = 96
EVENS = (TILES + 1) // 2
CHUNKS = 12
RING = 6
LEVELS = 7
HALF = S // 2

AT_FQ, AT_FK, AT_FV, AT_HQ, AT_HF, AT_HI, AT_HG, AT_PU = 0, 384, 768, 1158, 1542, 1926, 2310, 2694
VW = FOX + NH
VP = (NH - 1) * (HD + 1) + WIDE + 1
B_FQ, B_HQ, B_PU, B_FK, B_HF, B_HG = 0, 3, 6, 8, 11, 14
BLOCK_COLUMNS = ([AT_FQ + P * j for j in range(3)] + [AT_HQ + P * j for j in range(3)]
                 + [AT_PU + P * j for j in range(2)] + [AT_FK + P * j for j in range(3)]
                 + [AT_HF + P * j for j in range(3)] + [AT_HG + P * j for j in range(3)])
NB = len(BLOCK_COLUMNS)


class Chain:

    def __init__(self, eng, sem):
        self.eng, self.sem, self.n, self.base = eng, sem, 0, 0

    def __call__(self, ins):
        self.n += 1
        ins.then_inc(self.sem, 1)
        self.eng.wait_ge(self.sem, self.n + self.base)

    def enter(self, i, per):
        self.kept, self.per = self.n, per
        self.base = i * per

    def leave(self, times):
        assert self.n - self.kept == self.per, (self.n - self.kept, self.per)
        self.n, self.base = self.kept + self.per * times, 0


def copied_b(n):
    return n // 8 * 4 + max(n % 8 - 3, 0)


def build(nc, a, out):
    f2 = lambda ap: ap.rearrange("a d -> (a d)")

    x_v = a["x"][0].rearrange("(t p) d -> p t d", p=P)
    out_v = out[0].rearrange("(t p) d -> p t d", p=P)
    c_v = a["c"].rearrange("b (p k) -> p (b k)", k=K)
    ada_v = a["w_ada"][0].rearrange("(p k) (n e) -> n p k e", k=K, e=CH)
    win_v = a["w_in"][0].rearrange("(k p) n -> p k n", p=P)
    wout_v = a["w_out"][0].rearrange("(k p) n -> p k n", p=P)
    wg_v = a["expert_w_gate"][0].rearrange("e (k p) f -> e p k f", p=P)
    wu_v = a["expert_w_up"][0].rearrange("e (k p) f -> e p k f", p=P)
    wd_v = a["expert_w_down"][0].rearrange("e (k p) f -> e p k f", p=P)
    col = lambda ap: ap.rearrange("a (n p) -> p (a n)", p=P)

    f_rows = nc.dram_tensor("f_rows", [2, NH, S], F32, kind="Internal").ap()
    h2_rows = nc.dram_tensor("h2_rows", [S + P, D], F32, kind="Internal").ap()
    acc_rows = nc.dram_tensor("acc_rows", [S + P, D], F32, kind="Internal").ap()

    with ExitStack() as ctx:
        at = [16512]

        def put(name, shape, dt=F32, offset=None):
            size = 4
            for n in shape[1:]:
                size *= n
            o = offset
            if o is None:
                o = at[0]
                at[0] = (o + size + 31) // 32 * 32
            return nc.alloc_sbuf_tensor_at(name, shape, dt, offset=o)

        ident = put("ident", [P, P])
        ones = put("ones", [P, P])
        before = put("before", [P, P])
        causal = put("causal", [P, P])
        level_mask = put("level_mask", [P, LEVELS, P])
        c_raw = put("c_raw", [P, K])
        c_silu = put("c_silu", [P, K])
        waited = put("waited", [P, 16])
        waited_pool = put("waited_pool", [P, 4])
        ss = put("ss", [P, T])
        ms = put("ms", [P, T])
        rstd = put("rstd", [P, T])
        power = put("power", [P, 96])
        g1c = put("g1c", [P, K])
        scale1c = put("scale1c", [P, K])
        shift1c = put("shift1c", [P, K])
        foxg = put("foxg", [P, PAIRS])
        hgrng = put("hgrng", [P, PAIRS])
        lbl = put("lbl", [P, PAIRS])
        lbd = put("lbd", [P, PAIRS])
        lbe = put("lbe", [P, PAIRS])
        lbr = put("lbr", [P, PAIRS])
        lbp = put("lbp", [P, PAIRS])
        lb = put("lb", [P, PAIRS])
        oml = put("oml", [P, PAIRS])
        pscale = put("pscale", [P, 2])
        fbias = put("fbias", [P, NH])
        rbias = put("rbias", [P, G + E_ALL])
        gate = put("gate", [P, T, NH])
        gate_soft = put("gate_soft", [P, T, NH])
        log_forget = put("log_forget", [P, T, NH])
        nmax = put("nmax", [P, 2])
        pool_w = put("pool_w", [P, 2, P])
        wcol = put("wcol", [P, 2])
        iwcol = put("iwcol", [P, 2])
        invc = put("invc", [P, 2, 16])
        head_ss = put("head_ss", [P, 2, T * NH])
        head_ms = put("head_ms", [P, 2, T * NH])
        head_r = put("head_r", [P, 2, T * NH])
        rl = put("rl", [P, T * NH])
        el = put("el", [P, T])
        states = put("states", [P, T, P])
        logits = put("logits", [P, T, G + E_ALL])
        x_at = at[0]
        X = put("X", [P, T, D])
        mod = put("mod", [P, 2 * MOD_N, CH])
        mod_at = at[0] - 2 * MOD_N * CH * 4
        pt_at = at[0]
        PT = put("PT", [P, NB, S])
        va_at = at[0]
        VA = put("VA", [P, T, VP])
        HI = put("HI", [P, T, HG])
        r_at = at[0]
        end = 229344
        assert r_at + 45248 <= end, (r_at, end)
        ada = put("ada", [P, 2, K, CH], offset=pt_at)
        xhat = put("xhat", [P, T, D], offset=pt_at + 32768)
        junk = put("junk", [P, D], offset=pt_at + 65536)
        c_wide = put("c_wide", [P, K, P], offset=r_at + 32768)
        hT = put("hT", [P, K, S], offset=r_at)
        w_v = put("w_v", [P, K, VW], offset=pt_at)
        w_i = put("w_i", [P, K, HG], offset=pt_at + 4 * K * VW)
        w_t = put("w_t", [P, 3, K, P], offset=r_at + 32768)
        QA = [put(f"QA{e}", [P, S], offset=r_at + 8192 * e) for e in range(2)]
        KA = [put(f"KA{e}", [P, S], offset=r_at + 8192 * e + 4096) for e in range(2)]
        prob = put("prob", [P, 2, S], offset=r_at + 16384)
        probT = put("probT", [P, 2, T, P], offset=r_at + 24576)
        OF = put("OF", [P, T, NH, HD + 1], offset=r_at + 32768)
        f_sum = put("f_sum", [NH, S], offset=r_at + 16384)
        f_neg = put("f_neg", [NH, S], offset=r_at + 20480)
        ones_row = put("ones_row", [NH, S], offset=r_at + 24576)
        win_sum = put("win_sum", [P, 2, S], offset=mod_at)
        qb = put("qb", [P, S], offset=r_at)
        kb = put("kb", [P, S], offset=r_at + 4096)
        bsum = put("bsum", [P, S], offset=r_at + 8192)
        dec = put("dec", [P, 2, S], offset=r_at + 12288)
        gk = put("gk", [P, 2, S], offset=r_at + 20480)
        qe = put("qe", [P, S], offset=r_at + 28672)
        scores = put("scores", [P, 2, T, P], offset=pt_at + B_FK * 4096)
        carry = put("carry", [P, S], offset=pt_at + (B_FK + 2) * 4096)
        ke = [[put(f"ke{e}{b}", [P, S], offset=(pt_at + 4096 * (2 * e + b), mod_at + 4096)[e * b])
               for b in range(2)] for e in range(2)]
        kdT = put("kdT", [P, T, P], offset=mod_at)
        HO = put("HO", [P, T, NH, HD], offset=va_at)
        sq = put("sq", [P, T, NH, HD], offset=r_at)
        ON = put("ON", [P, T, NH, HD], offset=r_at + 12288)
        wo_a = put("wo_a", [P, 6, D], offset=pt_at + B_FK * 4096)
        wo_b = put("wo_b", [P, 2, D], offset=mod_at)
        ytmp = put("ytmp", [P, 2, D], offset=r_at)
        h2 = put("h2", [P, 2, D], offset=r_at + 8192)
        h2T = put("h2T", [P, 2, K, P], offset=r_at + 16384)
        junk2 = put("junk2", [P, D], offset=r_at + 24576)
        rw = put("rw", [P, K, WIDE], offset=r_at + 32768)
        zero_rows = put("zero_rows", [P, D], offset=r_at + 28672)
        g2 = put("g2", [P, D], offset=r_at + 40960)
        rt_at = [r_at]

        def small(name, shape, dt=F32):
            size = 4
            for n in shape[1:]:
                size *= n
            o = rt_at[0]
            rt_at[0] += (size + 31) // 32 * 32
            return put(name, shape, dt, offset=o)

        first4 = small("first4", [P, EG])
        gmax = small("gmax", [P, T])
        gdif = small("gdif", [P, T, G])
        gexp = small("gexp", [P, T, G])
        gsum = small("gsum", [P, T])
        pgroup = small("pgroup", [P, T])
        eqv = small("eqv", [P, T, 4])
        fst = small("fst", [P, T])
        oh_g = small("oh_g", [P, T, G])
        picked = small("picked", [P, T, EG, G])
        local = small("local", [P, T, EG])
        lmax = small("lmax", [P, T])
        oh_1 = small("oh_1", [P, T, EG])
        local2 = small("local2", [P, T, EG])
        lmax2 = small("lmax2", [P, T])
        oh_2 = small("oh_2", [P, T, EG])
        ldif = small("ldif", [P, T])
        lexp = small("lexp", [P, T])
        lden = small("lden", [P, T])
        lrec = small("lrec", [P, T])
        m1 = small("m1", [P, T, G, EG])
        m2 = small("m2", [P, T, G, EG])
        both = small("both", [P, T, E_ALL])
        rank = small("rank", [P, T, E_ALL])
        tot = small("tot", [P, T, E_ALL])
        run = small("run", [P, T + 1, E_ALL])
        hund = small("hund", [P, E_ALL, T])
        ntile = small("ntile", [P, E_ALL])
        tend = small("tend", [P, E_ALL])
        tbase = small("tbase", [P, E_ALL])
        pos = small("pos", [P, T, E_ALL])
        pick = small("pick", [P, T, E_ALL])
        slots = small("slots", [P, 2, T])
        step128 = small("step128", [P, T])
        tile_no = small("tile_no", [P, TILES])
        t_cmp = small("t_cmp", [P, TILES, E_ALL])
        t_exp = small("t_exp", [P, TILES])
        t_new = small("t_new", [P, TILES])
        token_row = small("token_row", [P, 2, T])
        lane = small("lane", [P, P])
        unused_row = small("unused_row", [P, 1])
        row_plus = small("row_plus", [P, TILES])
        unused = small("unused", [P, TILES])
        slot_lo = small("slot_lo", [P, 2 * T], U32)
        slot_hi = small("slot_hi", [P, 2 * T], U32)
        slot_lane = small("slot_lane", [P, 2 * T])
        slot_tile = small("slot_tile", [P, 2 * T])
        in_tile = small("in_tile", [P, 2 * T, TILES])
        lanes = small("lanes", [P, 2 * T, P])
        tiles = small("tiles", [P, 2 * T, WIDE])
        w12 = small("w12", [P, 2, T])
        slots_i = small("slots_i", [P, 2, T], U32)
        assert rt_at[0] <= end - 640, rt_at[0] - r_at
        t_exp_i = put("t_exp_i", [P, TILES], I32, offset=end - 128)
        t_new_i = put("t_new_i", [P, TILES], I32, offset=end - 512)
        slot_row = put("slot_row", [P, TILES + 1], U32, offset=end - 256)
        slot_w = put("slot_w", [P, TILES], offset=end - 384)
        mo = pt_at
        w_hi = put("w_hi", [P, RING, 2, FF], F32R, offset=x_at)
        w_lo = put("w_lo", [P, RING, 2, FF], F32R, offset=x_at + RING * 4096)
        XT_hi = put("XT_hi", [P, K, P], F32R, offset=x_at + 2 * RING * 4096)
        assert x_at + (2 * RING + 1) * 4096 <= mod_at + 10 * CH * 4
        wg = put("wg", [P, 2, K, FF], offset=mo)
        wu = put("wu", [P, 2, K, FF], offset=mo + 32768)
        wd = put("wd", [P, 2, FC, D], offset=mo + 65536)
        XG = put("XG", [P, 2, D], offset=mo + 98304)
        XT_lo = put("XT_lo", [P, K, P], F32R, offset=mo + 106496)
        hidT_hi = put("hidT_hi", [P, FC, P], F32R, offset=mo + 110592)
        hidT_lo = put("hidT_lo", [P, FC, P], F32R, offset=mo + 112640)
        sil = put("sil", [P, FF], offset=mo + 114688)
        hid = put("hid", [P, FF], offset=mo + 116736)
        Y = put("Y", [P, 2, D], offset=mo + 120832)
        row_in = put("row_in", [P, 2], U32, offset=mo + 129024)
        row_out = put("row_out", [P, 2], U32, offset=mo + 129056)
        assert mo + 129088 <= end - 640
        fin = put("fin", [P, 2, D], offset=mo + 16384)
        junk3 = put("junk3", [P, D], offset=mo + 24576)
        gf = put("gf", [P, D], offset=mo + 28672)

        PS = ctx.enter_context(nc.psum_tensor("PS", [P, 8, 512], F32))

        def sem(name):
            return ctx.enter_context(nc.semaphore(name))

        dve_step, pool_step, act_step = sem("dve_step"), sem("pool_step"), sem("act_step")
        (c_in, x_in, small_in, bada_in, win_v_in, rows_out, rows_in) = map(sem, (
            "c_in", "x_in", "small_in", "bada_in", "win_v_in", "rows_out", "rows_in"))
        ada_in = [sem(f"ada_in{s}") for s in range(2)]
        win_in = [sem(f"win_in{s}") for s in range(3)]
        (consts, silu_c, c_wide_up, ada_mm, ada_out, x_sq, x_hat, cols_mm, cols_up, tx_done,
         ht_act, ht_dve) = map(sem, (
            "consts", "silu_c", "c_wide_up", "ada_mm", "ada_out", "x_sq", "x_hat", "cols_mm",
            "cols_up", "tx_done", "ht_act", "ht_dve"))
        v_mm, va_out, hi_out, proj_mm, pt_act, pt_dve = map(sem, (
            "v_mm", "va_out", "hi_out", "proj_mm", "pt_act", "pt_dve"))
        (gate_up, gate_ln_up, lf_up, lf_T, f_up, silu_up, q_scaled, pooled_up,
         mod_up) = map(sem, (
            "gate_up", "gate_ln_up", "lf_up", "lf_T", "f_up", "silu_up", "q_scaled", "pooled_up",
            "mod_up"))
        qk_in = [sem(f"qk_in{e}") for e in range(2)]
        s_done, max_up, p_up, t_done, pta, ptb, pv_done, o_out = map(sem, (
            "s_done", "max_up", "p_up", "t_done", "pta", "ptb", "pv_done", "o_out"))
        (k_up, logf_up, b_up, q_up, qe_exp, qe_up, kd_d, kd_e, kd_up, kdT_mm, kdT_up, ds_mm, st_up,
         d_up, e_up, g_up, ke_up, lv_mm, sc_out, ho_mm, ho_out) = map(sem, (
            "k_up", "logf_up", "b_up", "q_up", "qe_exp", "qe_up", "kd_d", "kd_e", "kd_up",
            "kdT_mm", "kdT_up", "ds_mm", "st_up", "d_up", "e_up", "g_up", "ke_up", "lv_mm", "sc_out",
            "ho_mm", "ho_out"))
        pool_mm, pool_out, fsq_in, fsq, fss, frs, on_up, mT_mm, mT_act, mT_dve, wo_in = map(sem, (
            "pool_mm", "pool_out", "fsq_in", "fsq", "fss", "frs", "on_up", "mT_mm", "mT_act",
            "mT_dve", "wo_in"))
        (y_mm, y_gated, x2_up, x2_sq, h2_r, h2_m, h2_up, h2_T, h2T_up, rt_mm, rt_out,
         g2_in) = map(sem, (
            "y_mm", "y_gated", "x2_up", "x2_sq", "h2_r", "h2_m", "h2_up", "h2_T",
            "h2T_up", "rt_mm", "rt_out", "g2_in"))
        (r_exp_in, r_exp, masks_up, rank_mm, tiles_up, onehot_up, table_mm, table_up, iota_up,
         zero_up, unused_out, x2_out, rw_in) = map(sem, (
            "r_exp_in", "r_exp", "masks_up", "rank_mm", "tiles_up", "onehot_up", "table_mm",
            "table_up", "iota_up", "zero_up", "unused_out", "x2_out", "rw_in"))
        h2_out = [sem(f"h2_out{s}") for s in range(2)]
        g_in = [sem(f"g_in{s}") for s in range(2)]
        u_in = [sem(f"u_in{s}") for s in range(2)]
        d_in = [sem(f"d_in{s}") for s in range(2)]
        xg_in = [sem(f"xg_in{s}") for s in range(2)]
        y_out = [sem(f"y_out{s}") for s in range(2)]
        (xT_mm, xT_hi, xT_lo, g_mm, u_mm, sil_up, hid_up, hT_mm, hT_hi, hT_lo, dn_mm, hi_up, lo_dve,
         lo_pool, chunk_mm) = map(sem, (
            "xT_mm", "xT_hi", "xT_lo", "g_mm", "u_mm", "sil_up", "hid_up", "hT_mm", "hT_hi",
            "hT_lo", "dn_mm", "hi_up", "lo_dve", "lo_pool", "chunk_mm"))
        x3_in = [sem(f"x3_in{t}") for t in range(T)]
        fin_out = [sem(f"fin_out{s}") for s in range(2)]
        row_in_up, gathers, scatters, y_up = map(sem, ("row_in_up", "gathers", "scatters", "y_up"))
        gf_in, x3_sq, x3_up, x3_r, fin_up = map(sem, ("gf_in", "x3_sq", "x3_up", "x3_r", "fin_up"))

        N_SMALL = 12
        FINI = 2 * PAIRS * 2

        def tokens(t):
            return slice(t * P, (t + 1) * P)

        def weights(c, s):
            if c < 8:
                return (wg, wu)[c // 4][:, s, 2 * (c % 4):2 * (c % 4) + 2, :]
            return wd[:, s, c - 8, :].rearrange("p (k f) -> p k f", k=2)

        def heads(ap):
            return ap.rearrange("p t h d -> p (t h) d")

        block = ctx.enter_context(nc.Block())

        @block.sync
        def _(sp):
            sp.dma_start(c_raw[:], c_v).then_inc(c_in, 16)
            for s in range(2):
                sp.dma_start(ada[:, s], ada_v[s]).then_inc(ada_in[s], 16)
            sp.dma_start(X[:, 0:4], x_v[:, 0:4]).then_inc(x_in, 16)
            with sp.Fori(1, MOD_N) as i:
                for s in range(2):
                    sp.wait_ge(ada_mm, 2 * i - 1 + s)
                    sp.dma_start(ada[:, s], ada_v[2 * i + s]).then_inc(ada_in[s], 16)
            sp.wait_ge(ada_mm, 2 * MOD_N)
            sp.dma_start(w_v[:], win_v[:, :, AT_FV:AT_FV + VW]).then_inc(win_v_in, 16)
            sp.dma_start(w_i[:], win_v[:, :, AT_HI:AT_HI + HG]).then_inc(win_v_in, 16)
            for b, c0 in enumerate(BLOCK_COLUMNS):
                if b >= 3:
                    sp.wait_ge(proj_mm, 2 * b - 4)
                sp.dma_start(w_t[:, b % 3], win_v[:, :, c0:c0 + P]).then_inc(win_in[b % 3], 16)
            sp.wait_ge(f_up, 2)
            sp.dma_start(f_rows[0], f_sum[:]).then_inc(rows_out, 16)
            sp.dma_start(f_rows[1], f_neg[:]).then_inc(rows_out, 16)
            sp.wait_ge(rows_out, 32)
            sp.wait_ge(q_scaled, 4)

            def load_pair(i, first):
                for e in range(2):
                    if not first:
                        sp.wait_ge(s_done, 16 * i - 8 + 8 * e)
                    half = slice(HD * e, HD * (e + 1))
                    sp.dma_start(QA[e][0:HD, :], PT[half, B_FQ + i, :]).then_inc(qk_in[e], 16)
                    sp.dma_start(KA[e][0:HD, :], PT[half, B_FK + i, :]).then_inc(qk_in[e], 16)
                    sp.dma_start(QA[e][HD + 1:HD + 2, :], f_rows[0, bass.ds(2 * i + e, 1), :])\
                        .then_inc(qk_in[e], 16)
                    sp.dma_start(KA[e][HD:HD + 1, :], f_rows[1, bass.ds(2 * i + e, 1), :])\
                        .then_inc(qk_in[e], 16)

            load_pair(0, True)
            with sp.Fori(1, PAIRS) as i:
                load_pair(i, False)
            sp.wait_ge(ho_mm, PAIRS)
            sp.dma_start(wo_a[:], wout_v[:, 0:6, :]).then_inc(wo_in, 16)
            sp.dma_start(wo_b[:], wout_v[:, 6:8, :]).then_inc(wo_in, 16)
            sp.wait_ge(zero_up, 1)
            sp.dma_start(h2_rows[S:S + P, :], zero_rows[:]).then_inc(unused_out, 16)
            sp.dma_start(acc_rows[S:S + P, :], zero_rows[:]).then_inc(unused_out, 16)
            for t in range(T):
                sp.wait_ge(x2_up, t + 1)
                sp.dma_start(acc_rows[t * P:(t + 1) * P, :], X[:, t, :]).then_inc(x2_out, 16)
                sp.wait_ge(h2_up, t + 1)
                sp.dma_start(h2_rows[t * P:(t + 1) * P, :], h2[:, t % 2, :]).then_inc(h2_out[t % 2], 16)
            sp.wait_ge(tiles_up, 1)
            sp.wait_ge(rt_mm, T)

            def load_expert(j, s, first):
                e = sp.value_load(t_exp_i[0:1, bass.ds(j, 1)], min_val=0, max_val=E_ALL - 1)
                parts = ((wg, wg_v, g_in), (wu, wu_v, u_in), (wd, wd_v, d_in))

                def part_used(n):
                    sp.wait_ge(chunk_mm, CHUNKS * j - 2 * CHUNKS + 4 * n + 4)

                if first:
                    for w, src, done in parts:
                        sp.dma_start(w[:, s], src[e]).then_inc(done[s], 16)
                    return
                new = sp.value_load(t_new_i[0:1, bass.ds(j, 1)], min_val=0, max_val=1)
                with sp.If(new > 0):
                    for n, (w, src, done) in enumerate(parts):
                        part_used(n)
                        sp.dma_start(w[:, s], src[e]).then_inc(done[s], 16)
                with sp.Else():
                    for n, (w, src, done) in enumerate(parts):
                        part_used(n)
                        sp.nop().then_inc(done[s], 16)

            for s in range(2):
                load_expert(s, s, True)
            with sp.Fori(1, TILES // 2) as i:
                for s in range(2):
                    load_expert(2 * i + s, s, False)
            load_expert(TILES - 1, 0, False)
            for s in range(2):
                sp.wait_ge(y_out[s], 16 * ((TILES + 1 - s) // 2))
            for t in range(T):
                sp.dma_start(X[:, t, :], acc_rows[t * P:(t + 1) * P, :]).then_inc(x3_in[t], 16)
            for t in range(T):
                sp.wait_ge(fin_up, t + 1)
                sp.dma_start(out_v[:, t], fin[:, t % 2, :]).then_inc(fin_out[t % 2], 16)
            for s in range(2):
                sp.wait_ge(fin_out[s], 16 * T // 2)

        @block.tensor
        def _(pe):
            mm, tr = nc.tensor.matmul, nc.tensor.transpose
            pe.wait_ge(c_wide_up, 1)

            def ada_chunks(i, first):
                for s in range(2):
                    pe.wait_ge(ada_in[s], 16 * i + 16)
                    if not first:
                        pe.wait_ge(ada_out, 2 * i - 1 + s)
                    for k in range(K):
                        m = mm(PS[:, s, :], c_wide[:, k, :], ada[:, s, k, :],
                               start=(k == 0), stop=(k == K - 1))
                    m.then_inc(ada_mm, 1)

            ada_chunks(0, True)
            with pe.Fori(1, MOD_N) as i:
                ada_chunks(i, False)
            pe.wait_ge(consts, 1)
            pe.wait_ge(ada_out, 2 * MOD_N)
            for j in range(4):
                for q in range(4):
                    n = 4 * j + q
                    m = mm(PS[:, 2, n:n + 1], mod[0:1, j, q * P:(q + 1) * P], ones[0:1, 0:1],
                           start=True, stop=True)
            m.then_inc(cols_mm, 1)
            pe.wait_ge(x_hat, T)
            for j in range(2 * K):
                if j == 2:
                    pe.wait_ge(cols_up, 2)
                if j >= 8:
                    pe.wait_ge([ht_act, ht_dve][j % 2], (j - 8) // 2 + 1)
                for q in range(4):
                    m = tr(PS[:, j % 8, q * P:(q + 1) * P],
                           xhat[:, 4 * (j % 2) + q, (j // 2) * P:(j // 2 + 1) * P], ident[:])
                m.then_inc(tx_done, 1)
            pe.wait_ge(ht_act, K)
            pe.wait_ge(ht_dve, K)
            pe.wait_ge(win_v_in, 32)
            for t in range(T):
                b = 2 * t % 8
                if t >= 4:
                    pe.wait_ge(va_out, t - 3)
                    pe.wait_ge(hi_out, t - 3)
                for k in range(K):
                    mm(PS[:, b, 0:VW], hT[:, k, tokens(t)], w_v[:, k, :],
                       start=(k == 0), stop=(k == K - 1))
                for k in range(K):
                    m = mm(PS[:, b + 1, 0:HG], hT[:, k, tokens(t)], w_i[:, k, :],
                           start=(k == 0), stop=(k == K - 1))
                m.then_inc(v_mm, 1)
            pe.wait_ge(va_out, T)
            pe.wait_ge(hi_out, T)

            def proj_block(s, turn, b):
                pe.wait_ge(win_in[s], 16 * turn + 16)
                if b is not None:
                    pe.wait_ge(pt_act, b - 2)
                    pe.wait_ge(pt_dve, b - 2)
                for h in range(2):
                    for k in range(K):
                        m = mm(PS[:, 2 * s + h, :], w_t[:, s, k, :],
                               hT[:, k, h * HALF:(h + 1) * HALF], start=(k == 0), stop=(k == K - 1))
                    m.then_inc(proj_mm, 1)

            for s in range(3):
                proj_block(s, 0, None)
            with pe.Fori(1, NB // 3) as i:
                for s in range(3):
                    proj_block(s, i, 3 * i + s)
            for s in range(NB % 3):
                proj_block(s, NB // 3, NB // 3 * 3 + s)
            pe.wait_ge(lf_up, 1)
            for t in range(T):
                m = tr(PS[0:NH, 6 + t // 4, (t % 4) * P:(t % 4 + 1) * P], log_forget[:, t, :],
                       ident[:])
            m.then_inc(lf_T, 1)

            def fox_scores(i, n, first):
                e, q = n // 8, n % 8
                if q == 0:
                    pe.wait_ge(qk_in[e], 64 * i + 64)
                if not first or n >= 2:
                    pe.wait_ge(p_up, 16 * i + n - 1)
                w = (q + 1) * P
                for c in range((w + 511) // 512):
                    u = min(w - 512 * c, 512)
                    m = mm(PS[:, n % 2 * 2 + c, 0:u], QA[e][:, tokens(q)],
                           KA[e][:, 512 * c:512 * c + u], start=True, stop=True)
                m.then_inc(s_done, 1)

            def fox_transpose(i, n, first):
                q = n % 8
                pe.wait_ge(p_up, 16 * i + n + 1)
                if not first or n >= 1:
                    pe.wait_ge(pta, 16 * i + n)
                    if not first or n >= 5:
                        pe.wait_ge(ptb, 8 * i + copied_b(n - 1))
                for k in range(q + 1):
                    m = tr(PS[:, 4 + k // 4, (k % 4) * P:(k % 4 + 1) * P],
                           prob[:, n % 2, tokens(k)], ident[:])
                m.then_inc(t_done, 1)

            def fox_values(i, n, first):
                e, q = n // 8, n % 8
                pe.wait_ge(pta, 16 * i + n + 1)
                if q >= 4:
                    pe.wait_ge(ptb, 8 * i + copied_b(n))
                if not first or n >= 2:
                    pe.wait_ge(o_out, 16 * i + n - 1)
                for k in range(q + 1):
                    m = mm(PS[:, 6 + n % 2, 0:WIDE], probT[:, n % 2, k, :],
                           VA[:, k, bass.ds((2 * i + e) * (HD + 1), WIDE)],
                           start=(k == 0), stop=(k == q))
                m.then_inc(pv_done, 1)

            def fox_pair(i, first):
                for n in range(18):
                    if n < 16:
                        fox_scores(i, n, first)
                    if 1 <= n < 17:
                        fox_transpose(i, n - 1, first)
                    if n >= 2:
                        fox_values(i, n - 2, first)

            pe.wait_ge(f_up, 2)
            pe.wait_ge(consts, 1)
            fox_pair(0, True)
            with pe.Fori(1, PAIRS) as i:
                fox_pair(i, False)

            pe.wait_ge(pooled_up, 2)
            for b in range(2):
                for h in range(2):
                    m = mm(PS[:, 2 * b + h, :], pool_w[:, b, :],
                           PT[:, B_PU + b, h * HALF:(h + 1) * HALF], start=True, stop=True)
            m.then_inc(pool_mm, 1)
            pe.wait_ge(pool_out, 1)
            pe.wait_ge(o_out, 16 * PAIRS)

            def level_products(i, lv, lhs, rhs, first):
                for st in range(2):
                    r = 2 * lv + st
                    if not first or r >= 2:
                        pe.wait_ge(sc_out, 16 * i + r - 1)
                    for c in range(4):
                        for e in range(2):
                            tk = tokens(4 * st + c)
                            m = mm(PS[:, 2 * st + e, c * P:(c + 1) * P], lhs[e][:, tk],
                                   rhs[:, tk], start=True, stop=True)
                    m.then_inc(lv_mm, 1)

            def hgrn_pair(i, first):
                pe.wait_ge(k_up, i + 1)
                pe.wait_ge(q_up, i + 1)
                level_products(i, 0, (ke[0][1], ke[1][1]), qb, first)
                pe.wait_ge(kd_up, i + 1)
                if not first:
                    pe.wait_ge(ho_out, i)
                for c in range(T):
                    m = tr(PS[:, 4 + c // 4, (c % 4) * P:(c % 4 + 1) * P], dec[:, 0, tokens(c)],
                           ident[:])
                m.then_inc(kdT_mm, 1)
                for lv in range(LEVELS):
                    pe.wait_ge(g_up, LEVELS * i + lv + 1)
                    pe.wait_ge(ke_up, LEVELS * i + lv + 1)
                    level_products(i, lv + 1, (ke[0][lv % 2], ke[1][lv % 2]), gk[:, lv % 2, :],
                                   first)
                    if lv == 0:
                        pe.wait_ge(kdT_up, i + 1)
                        for c in range(T):
                            m = mm(PS[:, 6 + c // 4, (c % 4) * P:(c % 4 + 1) * P], kdT[:, c, :],
                                   HI[:, c, bass.ds(P * i, P)], start=True, stop=True)
                        m.then_inc(ds_mm, 1)
                pe.wait_ge(qe_up, i + 1)
                pe.wait_ge(st_up, i + 1)
                pe.wait_ge(sc_out, 16 * i + 16)
                for c in range(T):
                    o = PS[:, 4 + c // 4, c % 4 * P:(c % 4 + 1) * P]
                    mm(o, qe[:, tokens(c)], states[:, c, :], start=True, stop=False)
                    for e in range(2):
                        m = mm(o[:, HD * e:HD * (e + 1)], scores[:, e, c, :],
                               HI[:, c, bass.ds(P * i + HD * e, HD)], start=False, stop=(e == 1))
                m.then_inc(ho_mm, 1)

            hgrn_pair(0, True)
            with pe.Fori(1, PAIRS) as i:
                hgrn_pair(i, False)

            for j in range(2 * FINI // 2):
                g, r = j // (2 * PAIRS), j % (2 * PAIRS)
                src = (ON, HO)[g]
                if r == 0:
                    pe.wait_ge(on_up, g + 1)
                    if g == 0:
                        pe.wait_ge(ho_out, PAIRS)
                if j >= 8:
                    pe.wait_ge([mT_act, mT_dve][j % 2], (j - 8) // 2 + 1)
                for q in range(4):
                    t = 4 * (r % 2) + q
                    pair = r // 2
                    m = tr(PS[:, j % 8, q * P:(q + 1) * P],
                           src[:, t, 2 * pair:2 * pair + 2, :].rearrange("p h d -> p (h d)"),
                           ident[:])
                m.then_inc(mT_mm, 1)

            pe.wait_ge(wo_in, 32)
            pe.wait_ge(mT_act, 2 * PAIRS)
            pe.wait_ge(mT_dve, 2 * PAIRS)
            pe.wait_ge(mod_up, 1)
            pe.wait_ge(rw_in, 32)

            def router(t):
                pe.wait_ge(h2_up, t + 1)
                if t >= 1:
                    pe.wait_ge(h2T_up, t)
                for k in range(K):
                    m = tr(PS[:, 4 + k // 4, (k % 4) * P:(k % 4 + 1) * P],
                           h2[:, t % 2, k * P:(k + 1) * P], ident[:])
                m.then_inc(h2_T, 1)
                pe.wait_ge(h2T_up, t + 1)
                if t >= 1:
                    pe.wait_ge(rt_out, t)
                for k in range(K):
                    m = mm(PS[:, 6, 0:WIDE], h2T[:, t % 2, k, :], rw[:, k, :],
                           start=(k == 0), stop=(k == K - 1))
                m.then_inc(rt_mm, 1)

            for t in range(T):
                if t >= 2:
                    pe.wait_ge(y_gated, t - 1)
                for k in range(K):
                    w = wo_a[:, k, :] if k < 6 else wo_b[:, k - 6, :]
                    for h in range(2):
                        m = mm(PS[:, t % 2 * 2 + h, :], PT[:, k, tokens(t)],
                               w[:, h * CH:(h + 1) * CH], start=(k == 0), stop=(k == K - 1))
                m.then_inc(y_mm, 1)
                if t >= 1:
                    router(t - 1)
            router(T - 1)

            pe.wait_ge(masks_up, 1)
            mm(PS[:, 0, 0:T * E_ALL], before[:], both[:].rearrange("p t e -> p (t e)"),
               start=True, stop=True)
            mm(PS[:, 1, 0:T * E_ALL], ones[:], both[:].rearrange("p t e -> p (t e)"),
               start=True, stop=True).then_inc(rank_mm, 1)
            pe.wait_ge(onehot_up, 1)
            for n in range(2 * T):
                m = mm(PS[:, 2, 0:WIDE], lanes[:, n, :], tiles[:, n, :],
                       start=(n == 0), stop=(n == 2 * T - 1))
            m.then_inc(table_mm, 1)

            def turn_x(j, s, turn, half):
                if half == 0:
                    pe.wait_ge(xg_in[s], 16 * turn + 16)
                if not isinstance(j, int) or j >= 1:
                    pe.wait_ge(xT_lo, 2 * j - 1 + half)
                for k in range(4 * half, 4 * half + 4):
                    m = tr(PS[:, half, (k % 4) * P:(k % 4 + 1) * P],
                           XG[:, s, k * P:(k + 1) * P], ident[:])
                m.then_inc(xT_mm, 1)

            def chunk_split(j, c):
                if c % 4 == 3:
                    pe.wait_ge(lo_pool, 3 * j + c // 4 + 1)
                else:
                    pe.wait_ge(lo_dve, 9 * j + c - c // 4 + 1)

            def expert(i, s, first, last):
                j = 2 * i + s
                pe.wait_ge(xT_lo, 2 * j + 2)
                if not first:
                    pe.wait_ge(sil_up, j)
                for c in range(8):
                    chunk_split(j, c)
                    if c == 4 and not first:
                        pe.wait_ge(hid_up, j)
                    o = PS[:, 2 + c // 4, :]
                    for n in range(2):
                        k = 2 * (c % 4) + n
                        hi, lo = w_hi[:, c % RING, n, :], w_lo[:, c % RING, n, :]
                        mm(o, XT_hi[:, k, :], hi, start=(k == 0), stop=False)
                        mm(o, XT_hi[:, k, :], lo, start=False, stop=False)
                        m = mm(o, XT_lo[:, k, :], hi, start=False, stop=(k == K - 1))
                    m.then_inc(chunk_mm, 1)
                if not last:
                    turn_x(j + 1, 1 - s, i + s, 0)
                pe.wait_ge(hid_up, j + 1)
                if not first:
                    pe.wait_ge(hT_lo, j)
                for k in range(FC):
                    m = tr(PS[:, 4, k * P:(k + 1) * P], hid[:, k * P:(k + 1) * P], ident[:])
                m.then_inc(hT_mm, 1)
                if not last:
                    turn_x(j + 1, 1 - s, i + s, 1)
                pe.wait_ge(hT_hi, j + 1)
                if not first:
                    pe.wait_ge(y_up, j)
                for c in range(8, CHUNKS):
                    chunk_split(j, c)
                    k = c - 8
                    for h in range(2):
                        o = PS[:, 5 + h, :]
                        mm(o, hidT_hi[:, k, :], w_hi[:, c % RING, h, :], start=(k == 0), stop=False)
                        mm(o, hidT_hi[:, k, :], w_lo[:, c % RING, h, :], start=False, stop=False)
                    if k == 0:
                        pe.wait_ge(hT_lo, j + 1)
                    for h in range(2):
                        m = mm(PS[:, 5 + h, :], hidT_lo[:, k, :], w_hi[:, c % RING, h, :],
                               start=False, stop=(k == FC - 1))
                    m.then_inc(chunk_mm, 1)

            for half in range(2):
                turn_x(0, 0, 0, half)
            expert(0, 0, True, False)
            expert(0, 1, False, False)
            with pe.Fori(1, TILES // 2) as i:
                for s in range(2):
                    expert(i, s, False, False)
            expert(TILES // 2, 0, False, True)

        @block.scalar
        def _(act):
            A = nc.scalar.activation
            act.dma_start(X[:, 4:8], x_v[:, 4:8]).then_inc(x_in, 16)
            act.dma_start(mod[:].rearrange("p n e -> p (n e)"),
                          a["b_ada"].partition_broadcast(P).rearrange("p a e -> p (a e)"))\
                .then_inc(bada_in, 16)
            act.wait_ge(consts, 1)
            for dst, src in ((g1c[:], col(a["norm1_g"])), (foxg[:], col(a["fox_norm_g"])),
                             (hgrng[:], col(a["hgrn_norm_g"])), (lbl[:], col(a["hgrn_lb_logits"])),
                             (pscale[:], col(a["pool_scale"])),
                             (fbias[:], a["fox_f_bias"].partition_broadcast(P).rearrange("p a e -> p (a e)")),
                             (rbias[:, 0:G], a["router_group_b"].partition_broadcast(P).rearrange("p a e -> p (a e)")),
                             (rbias[:, G:], a["router_expert_b"].partition_broadcast(P).rearrange("p a e -> p (a e)"))):
                act.dma_start(dst, src, allow_slow_non_contiguous=True).then_inc(small_in, 16)
            for g in range(4):
                r = slice(HD * (g % 2), HD * (g % 2 + 1))
                act.dma_start(pool_w[r, g // 2, r], a["pool_w"][0, g]).then_inc(small_in, 16)
            act.wait_ge(c_in, 16)
            A(c_silu[:], c_raw[:], ACT.Silu).then_inc(silu_c, 1)
            act.wait_ge(x_in, 32)
            for t in range(T):
                if t >= 1:
                    act.wait_ge(x_sq, t)
                A(junk[:], X[:, t, :], ACT.Square, accum_out=ss[:, t:t + 1]).then_inc(x_sq, 1)
            act.wait_ge(cols_up, 2)
            for j in range(0, 2 * K, 2):
                act.wait_ge(tx_done, j + 1)
                k = j // 2
                A(hT[:, k, 0:HALF], PS[:, j % 8, :], ACT.Identity, bias=shift1c[:, k:k + 1],
                  scale=scale1c[:, k:k + 1]).then_inc(ht_act, 1)
            act.wait_ge(consts, 1)
            for t in range(T):
                act.wait_ge(v_mm, t + 1)
                A(VA[:, t, 0:NH * (HD + 1)].rearrange("p (h d) -> p h d", h=NH)[:, :, 0:HD], PS[:, 2 * t % 8, 0:FOX].rearrange("p (h d) -> p h d", d=HD),
                  ACT.Copy).then_inc(va_out, 1)

            def proj_copy(b):
                act.wait_ge(proj_mm, 2 * b + 1)
                A(PT[:, b, 0:HALF], PS[:, 2 * s, :], ACT.Copy).then_inc(pt_act, 1)

            with act.Fori(0, NB // 3) as i:
                for s in range(3):
                    proj_copy(3 * i + s)
            for s in range(NB % 3):
                proj_copy(NB // 3 * 3 + s)
            act.wait_ge(pt_act, NB)
            act.wait_ge(pt_dve, NB)
            A(PT[:, B_HQ:B_HQ + 3, :], PT[:, B_HQ:B_HQ + 3, :], ACT.Silu).then_inc(silu_up, 1)
            A(PT[:, B_HG:B_HG + 3, :], PT[:, B_HG:B_HG + 3, :], ACT.Silu).then_inc(silu_up, 1)
            A(PT[:, B_HF:B_HF + 3, :], PT[:, B_HF:B_HF + 3, :], ACT.Sigmoid).then_inc(silu_up, 1)
            act.wait_ge(gate_up, 1)
            A(gate_soft[:], gate_soft[:], ACT.Exp, scale=-1.0).then_inc(act_step, 1)
            act.wait_ge(act_step, 1)
            A(gate_soft[:], gate_soft[:], ACT.Ln, bias=1.0).then_inc(gate_ln_up, 1)
            A(lbe[:], lbd[:], ACT.Exp).then_inc(gate_ln_up, 1)

            def fox_pair(i, first):
                for n in range(18):
                    if 1 <= n < 17:
                        m = n - 1
                        act.wait_ge(t_done, 16 * i + m + 1)
                        if not first or m >= 2:
                            act.wait_ge(pv_done, 16 * i + m - 1)
                        w = min(m % 8 + 1, 4)
                        A(probT[:, m % 2, 0:w, :].rearrange("p k q -> p (k q)"),
                          PS[:, 4, 0:w * P], ACT.Copy).then_inc(pta, 1)
                    if n < 16:
                        act.wait_ge(max_up, 16 * i + n + 1)
                        if not first or n >= 2:
                            act.wait_ge(t_done, 16 * i + n - 1)
                        w = (n % 8 + 1) * P
                        src = PS[:, n % 2 * 2:n % 2 * 2 + 2, :].rearrange("p b e -> p (b e)")
                        A(prob[:, n % 2, 0:w], src[:, 0:w], ACT.Exp,
                          bias=nmax[:, n % 2:n % 2 + 1]).then_inc(p_up, 1)
                    if n >= 2:
                        m = n - 2
                        act.wait_ge(pv_done, 16 * i + m + 1)
                        A(OF[:, m % 8, 2 * i + m // 8, :], PS[:, 6 + m % 2, 0:HD + 1],
                          ACT.Copy).then_inc(o_out, 1)

            fox_pair(0, True)
            with act.Fori(1, PAIRS) as i:
                fox_pair(i, False)

            act.wait_ge(pool_mm, 1)
            for b in range(2):
                m = A(PT[:, B_PU + b, :], PS[:, 2 * b:2 * b + 2, :].rearrange("p b e -> p (b e)"),
                      ACT.Copy, scale=pscale[:, b:b + 1])
            m.then_inc(pool_out, 1)

            def hgrn_pair(i, first):
                act.wait_ge(k_up, i + 1)
                A(dec[:, 1, :], dec[:, 0, :], ACT.Ln).then_inc(logf_up, 1)
                act.wait_ge(b_up, i + 1)
                ends = bsum[:].rearrange("p (c t) -> p c t", t=P)[:, :, P - 1]
                A(el[:], ends, ACT.Exp)
                if not first:
                    act.wait_ge(ho_mm, i)
                A(qe[:], bsum[:], ACT.Exp).then_inc(qe_exp, 1)
                act.wait_ge(kd_d, i + 1)
                A(dec[:, 0, :], dec[:, 0, :], ACT.Exp, scale=-1.0).then_inc(kd_e, 1)
                def level(ap, lv):
                    return ap.rearrange("p (n h t) -> p n h t", h=2, t=P >> (lv + 1))

                def heads_apart(lv):
                    act.wait_ge(g_up, LEVELS * i + lv + 1)
                    if lv >= 1 or not first:
                        act.wait_ge(lv_mm, 16 * i + 2 * lv)
                    for e in range(2):
                        r = slice(HD * e, HD * (e + 1))
                        m = A(level(ke[e][lv % 2][r, :], lv)[:, :, 0, :],
                              level(dec[r, (lv + 1) % 2, :], lv)[:, :, 0, :], ACT.Copy)
                    m.then_inc(ke_up, 1)

                for lv in range(LEVELS):
                    act.wait_ge(d_up, LEVELS * i + lv + 1)
                    v = level(dec[:, (lv + 1) % 2, :], lv)
                    A(v[:, :, 1, :], v[:, :, 1, :], ACT.Exp)
                    A(v[:, :, 0, :], v[:, :, 0, :], ACT.Exp, scale=-1.0).then_inc(e_up, 1)
                    if lv >= 1:
                        heads_apart(lv - 1)
                    if lv == 0:
                        act.wait_ge(kdT_mm, i + 1)
                        if not first:
                            act.wait_ge(ds_mm, i)
                        A(kdT[:].rearrange("p c t -> p (c t)"),
                          PS[:, 4:6, :].rearrange("p b e -> p (b e)"), ACT.Copy).then_inc(kdT_up, 1)
                heads_apart(LEVELS - 1)
                act.wait_ge(ho_mm, i + 1)
                A(HO[:, :, bass.ds(2 * i, 2), :],
                  PS[:, 4:6, :].rearrange("p b (c e d) -> p (b c) e d", e=2, d=HD),
                  ACT.Copy).then_inc(ho_out, 1)

            hgrn_pair(0, True)
            with act.Fori(1, PAIRS) as i:
                hgrn_pair(i, False)
            act.wait_ge(ho_out, PAIRS)
            for g, src in enumerate((ON, HO)):
                act.wait_ge(fsq_in, g + 1)
                A(heads(sq[:]), heads(src[:]), ACT.Square).then_inc(fsq, 1)
            for j in range(0, 4 * PAIRS, 2):
                act.wait_ge(mT_mm, j + 1)
                g, r = j // (2 * PAIRS), j % (2 * PAIRS)
                if g == 0:
                    A(PT[:, r // 2, 0:HALF], PS[:, j % 8, :], ACT.Copy,
                      scale=foxg[:, r // 2:r // 2 + 1]).then_inc(mT_act, 1)
                else:
                    A(PT[:, B_HQ + r // 2, 0:HALF], PS[:, j % 8, :], ACT.Copy,
                      scale=hgrng[:, r // 2:r // 2 + 1]).then_inc(mT_act, 1)
            act.wait_ge(mT_mm, 4 * PAIRS)

            def h2_turned(t):
                act.wait_ge(h2_T, t + 1)
                if t >= 2:
                    act.wait_ge(rt_mm, t - 1)
                A(h2T[:, t % 2].rearrange("p k q -> p (k q)"),
                  PS[:, 4:6, :].rearrange("p b e -> p (b e)"), ACT.Copy).then_inc(h2T_up, 1)

            for t in range(T):
                act.wait_ge(x2_up, t + 1)
                if t >= 1:
                    act.wait_ge(x2_sq, t)
                A(junk2[:], X[:, t, :], ACT.Square, accum_out=ss[:, t:t + 1]).then_inc(x2_sq, 1)
                if t >= 1:
                    h2_turned(t - 1)
            h2_turned(T - 1)
            act.wait_ge(r_exp_in, 1)
            A(gexp[:], gdif[:], ACT.Exp).then_inc(r_exp, 1)
            act.wait_ge(r_exp_in, 2)
            A(lexp[:], ldif[:], ACT.Exp).then_inc(r_exp, 1)

            act.wait_ge(x2_out, 16 * T)
            act.wait_ge(table_up, 1)

            def hi_chunk(j, c, s, i):
                if c % 4 == 0:
                    act.wait_ge((g_in, u_in, d_in)[c // 4][s], 16 * i + 16)
                if not isinstance(j, int) or CHUNKS * j + c >= RING:
                    act.wait_ge(chunk_mm, CHUNKS * j + c - RING + 1)
                A(w_hi[:, c % RING], weights(c, s), ACT.Copy).then_inc(hi_up, 1)

            def x_hi(j, half):
                act.wait_ge(xT_mm, 2 * j + half + 1)
                A(XT_hi[:, 4 * half:4 * half + 4, :].rearrange("p k q -> p (k q)"),
                  PS[:, half, :], ACT.Copy).then_inc(xT_hi, 1)

            def expert(i, s, first, last):
                j = 2 * i + s
                for c in range(4, 8):
                    hi_chunk(j, c, s, i)
                act.wait_ge(chunk_mm, CHUNKS * j + 4)
                if not first:
                    act.wait_ge(hid_up, j)
                A(sil[:], PS[:, 2, :], ACT.Silu).then_inc(sil_up, 1)
                for c in range(8, CHUNKS):
                    hi_chunk(j, c, s, i)
                if not last:
                    x_hi(j + 1, 0)
                act.wait_ge(hT_mm, j + 1)
                A(hidT_hi[:].rearrange("p k q -> p (k q)"), PS[:, 4, :], ACT.Copy).then_inc(hT_hi, 1)
                if not last:
                    x_hi(j + 1, 1)
                    for c in range(4):
                        hi_chunk(j + 1, c, 1 - s, i + s)

            for half in range(2):
                x_hi(0, half)
            for c in range(4):
                hi_chunk(0, c, 0, 0)
            expert(0, 0, True, False)
            expert(0, 1, False, False)
            with act.Fori(1, TILES // 2) as i:
                for s in range(2):
                    expert(i, s, False, False)
            expert(TILES // 2, 0, False, True)
            act.wait_ge(chunk_mm, CHUNKS * TILES)
            act.dma_start(gf[:], a["final_norm_g"].partition_broadcast(P)).then_inc(gf_in, 16)
            for t in range(T):
                act.wait_ge(x3_in[t], 16)
                if t >= 1:
                    act.wait_ge(x3_sq, t)
                A(junk3[:], X[:, t, :], ACT.Square, accum_out=ss[:, t:t + 1]).then_inc(x3_sq, 1)

        @block.vector
        def _(v):
            V = nc.vector
            step = Chain(v, dve_step)
            v.wait_ge(silu_c, 1)
            V.tensor_copy(c_wide[:], c_silu[:].unsqueeze(2).broadcast_to([P, K, P]))\
                .then_inc(c_wide_up, 1)
            v.wait_ge(bada_in, 16)
            with v.Fori(0, MOD_N) as i:
                for s in range(2):
                    v.wait_ge(ada_mm, 2 * i + s + 1)
                    V.tensor_tensor(mod[:, 2 * i + s, :], PS[:, s, :], mod[:, 2 * i + s, :],
                                    ALU.add).then_inc(ada_out, 1)
            v.wait_ge(small_in, 16 * N_SMALL)
            v.wait_ge(cols_mm, 1)
            V.scalar_tensor_tensor(scale1c[:], PS[:, 2, K:2 * K], 1.0, g1c[:], ALU.add,
                                   ALU.mult).then_inc(cols_up, 1)
            V.tensor_copy(shift1c[:], PS[:, 2, 0:K]).then_inc(cols_up, 1)
            v.wait_ge(cols_up, 2)
            for j in range(1, 2 * K, 2):
                v.wait_ge(tx_done, j + 1)
                k = j // 2
                V.tensor_scalar(hT[:, k, HALF:S], PS[:, j % 8, :], scale1c[:, k:k + 1],
                                shift1c[:, k:k + 1], ALU.mult, ALU.add).then_inc(ht_dve, 1)
            v.wait_ge(ada_out, 2 * MOD_N)
            for n in (4, 8, 10):
                step(V.tensor_scalar(mod[:, n:n + 2, :], mod[:, n:n + 2, :], 1.0, None, ALU.add))
            step(V.tensor_tensor(lbd[:], lbl[:], lbl[:], ALU.subtract))
            for t in range(T):
                v.wait_ge(v_mm, t + 1)
                v.wait_ge(va_out, t + 1)
                b = 2 * t % 8
                V.tensor_tensor(gate[:, t, :], PS[:, b, FOX:VW], fbias[:], ALU.add)
                V.tensor_copy(HI[:, t, :], PS[:, b + 1, 0:HG]).then_inc(hi_out, 1)
            v.wait_ge(hi_out, T)
            V.scalar_tensor_tensor(gate_soft[:], gate[:], -1.0, gate[:], ALU.mult, ALU.max)\
                .then_inc(gate_up, 1)

            def proj_copy(b, s):
                v.wait_ge(proj_mm, 2 * b + 2)
                V.tensor_copy(PT[:, b, HALF:S], PS[:, 2 * s + 1, :]).then_inc(pt_dve, 1)

            with v.Fori(0, NB // 3) as i:
                for s in range(3):
                    proj_copy(3 * i + s, s)
            for s in range(NB % 3):
                proj_copy(NB // 3 * 3 + s, s)
            v.wait_ge(gate_ln_up, 2)
            V.scalar_tensor_tensor(log_forget[:], gate[:], 0.0, gate_soft[:], ALU.min,
                                   ALU.subtract).then_inc(lf_up, 1)
            step(V.memset(ones_row[:], 1.0))
            v.wait_ge(lf_T, 1)
            V.tensor_tensor_scan(f_sum[:], ones_row[:],
                                 PS[0:NH, 6:8, :].rearrange("p b e -> p (b e)"), 0.0, ALU.mult,
                                 ALU.add).then_inc(f_up, 1)
            v.wait_ge(f_up, 1)
            V.tensor_scalar(f_neg[:], f_sum[:], -1.0, None, ALU.mult).then_inc(f_up, 1)
            step(V.reciprocal(lbr[:], lbe[:]))
            step(V.tensor_tensor(lbp[:], lbe[:], lbr[:], ALU.mult))
            step(V.tensor_tensor(lb[:], lbp[:], lbp[:], ALU.subtract))
            step(V.tensor_scalar(oml[:], lb[:], -1.0, 1.0, ALU.mult, ALU.add))

            def fox_pair(i, first):
                step.enter(i, 16)
                for n in range(17):
                    if n < 16:
                        q = n % 8
                        v.wait_ge(s_done, 16 * i + n + 1)
                        dg = PS[:, n % 2 * 2 + q // 4, q % 4 * P:(q % 4 + 1) * P]
                        step(V.tensor_tensor(dg, dg, causal[:], ALU.add))
                        src = PS[:, n % 2 * 2:n % 2 * 2 + 2, :].rearrange("p b e -> p (b e)")
                        V.tensor_reduce(nmax[:, n % 2:n % 2 + 1], src[:, 0:(q + 1) * P], AX.X,
                                        ALU.max, negate=True).then_inc(max_up, 1)
                    m = n - 1
                    if n >= 1 and m % 8 >= 4:
                        v.wait_ge(t_done, 16 * i + m + 1)
                        v.wait_ge(pv_done, 16 * i + m - 1)
                        w = m % 8 - 3
                        V.tensor_copy(probT[:, m % 2, 4:4 + w, :].rearrange("p k q -> p (k q)"),
                                      PS[:, 5, 0:w * P]).then_inc(ptb, 1)

            v.wait_ge(consts, 1)
            v.wait_ge(rows_out, 32)
            fox_pair(0, True)
            step.leave(1)
            keep = step.n
            step.n = keep - 16
            with v.Fori(1, PAIRS) as i:
                fox_pair(i, False)
            step.leave(PAIRS)

            v.wait_ge(silu_up, 3)
            v.wait_ge(s_done, 16 * PAIRS)
            v.wait_ge(pv_done, 16 * PAIRS)
            v.wait_ge(pool_out, 1)
            v.wait_ge(qk_in[0], 64 * PAIRS)
            v.wait_ge(qk_in[1], 64 * PAIRS)
            step(V.memset(scores[:].rearrange("p e c t -> p (e c t)"), 0.0))
            step(V.memset(states[:].rearrange("p c e -> p (c e)"), 0.0))
            for e in range(2):
                for b in range(2):
                    step(V.memset(ke[e][b][:], 0.0))
                step(V.memset(gk[:, e, :], 0.0))
            step(V.memset(carry[:], 1.0))
            step(V.memset(carry[:].rearrange("p (c t) -> p c t", t=P)[:, :, 0:1], 0.0))
            bc = bsum[:].rearrange("p (c t) -> p c t", t=P)

            def level(i, lv, first):
                half = P >> (lv + 1)
                b = bsum[:].rearrange("p (n h t) -> p n h t", h=2, t=half)
                d = dec[:, (lv + 1) % 2, :].rearrange("p (n h t) -> p n h t", h=2, t=half)
                m = b[:, :, 0, half - 1:half].unsqueeze(2).broadcast_to([P, S // (2 * half), 2, half])
                if lv == 1:
                    v.wait_ge(kdT_mm, i + 1)
                if lv >= 2:
                    v.wait_ge(ke_up, LEVELS * i + lv - 1)
                V.tensor_tensor(d, b, m, ALU.subtract).then_inc(d_up, 1)

            def merge_level(i, lv, mask):
                for st in range(2):
                    v.wait_ge(lv_mm, 16 * i + 2 * lv + st + 1)
                    V.memset(waited[:, 2 * lv + st:2 * lv + st + 1], 0.0)
                    for e in range(2):
                        m = V.copy_predicated(
                            scores[:, e, 4 * st:4 * st + 4, :],
                            mask.bitcast(U32).unsqueeze(1).broadcast_to([P, 4, P]),
                            PS[:, 2 * st + e, :].rearrange("p (c t) -> p c t", t=P))
                    m.then_inc(sc_out, 1)

            def hgrn_pair(i, first):
                step.enter(i, 9)
                if not first:
                    v.wait_ge(ke_up, LEVELS * i)
                    v.wait_ge(ho_mm, i)
                step(V.tensor_scalar(dec[:, 0, :], PT[:, B_HF + i, :], oml[:, bass.ds(i, 1)],
                                     lb[:, bass.ds(i, 1)], ALU.mult, ALU.add))
                step(V.tensor_scalar(dec[:, 0, :], dec[:, 0, :], 1e-19, None, ALU.max))
                for e in range(2):
                    r = slice(HD * e, HD * (e + 1))
                    V.tensor_scalar(ke[e][1][r, :], dec[r, 0, :], -1.0, 1.0, ALU.mult, ALU.add)
                V.tensor_scalar(kb[:], dec[:, 0, :], -1.0, 1.0, ALU.mult, ALU.add)\
                    .then_inc(k_up, 1)
                v.wait_ge(logf_up, i + 1)
                V.tensor_tensor_scan(bsum[:], carry[:], dec[:, 1, :], 0.0, ALU.mult, ALU.add)\
                    .then_inc(b_up, 1)
                v.wait_ge(b_up, i + 1)
                V.tensor_tensor(dec[:, 0, :].rearrange("p (c t) -> p c t", t=P), bc,
                                bc[:, :, P - 1:P].broadcast_to([P, T, P]),
                                ALU.subtract).then_inc(kd_d, 1)
                level(i, 0, first)
                merge_level(i, 0, ident[:])
                for lv in range(LEVELS):
                    if lv + 1 < LEVELS:
                        level(i, lv + 1, first)
                    merge_level(i, lv + 1, level_mask[:, lv, :])
                    if lv == 0:
                        v.wait_ge(ds_mm, i + 1)
                        v.wait_ge(qe_exp, i + 1)
                        for c in range(1, T):
                            for e in range(2):
                                half = slice(HD * e, HD * (e + 1))
                                o = (c - 1) % 4 * P + HD * e
                                ds = PS[half, 6 + (c - 1) // 4, o:o + HD]
                                own = slice(HD * e, HD * (e + 1))
                                if c == 1:
                                    m = V.tensor_copy(states[half, c, own], ds)
                                else:
                                    m = V.scalar_tensor_tensor(
                                        states[half, c, own], states[half, c - 1, own],
                                        el[half, c - 1:c], ds, ALU.mult, ALU.add)
                            if c < T - 1:
                                step(m)
                        m.then_inc(st_up, 1)
                step(V.memset(rl[:, 0:1], 0.0))

            hgrn_pair(0, True)
            step.leave(1)
            step.n -= 9
            with v.Fori(1, PAIRS) as i:
                hgrn_pair(i, False)
            step.leave(PAIRS)
            v.wait_ge(ho_mm, PAIRS)
            v.wait_ge(o_out, 16 * PAIRS)
            of = heads(OF[:])
            step(V.reciprocal(rl[:], of[:, :, HD]))
            V.tensor_tensor(heads(ON[:]), of[:, :, 0:HD],
                            rl[:].unsqueeze(2).broadcast_to([P, T * NH, HD]),
                            ALU.mult).then_inc(fsq_in, 1)
            for g, src in enumerate((ON, HO)):
                v.wait_ge(fsq, g + 1)
                V.tensor_reduce(head_ss[:, g, :], heads(sq[:]), AX.X, ALU.add).then_inc(fss, 1)
                if g == 0:
                    v.wait_ge(ho_out, PAIRS)
                    v.wait_ge(fss, 1)
                    V.memset(rl[:, 0:1], 0.0).then_inc(fsq_in, 1)
                v.wait_ge(frs, g + 1)
                V.tensor_tensor(heads(src[:]), heads(src[:]),
                                head_r[:, g, :].unsqueeze(2).broadcast_to([P, T * NH, HD]),
                                ALU.mult).then_inc(on_up, 1)
            for j in range(1, 4 * PAIRS, 2):
                v.wait_ge(mT_mm, j + 1)
                g, r = j // (2 * PAIRS), j % (2 * PAIRS)
                gain, blk = ((foxg, 0), (hgrng, B_HQ))[g]
                V.tensor_scalar(PT[:, blk + r // 2, HALF:S], PS[:, j % 8, :],
                                gain[:, r // 2:r // 2 + 1], None, ALU.mult).then_inc(mT_dve, 1)
            v.wait_ge(mT_act, 2 * PAIRS)
            v.wait_ge(mT_dve, 2 * PAIRS)
            V.tensor_tensor(PT[:, B_HQ:B_HQ + 3, :], PT[:, B_HQ:B_HQ + 3, :],
                            PT[:, B_HG:B_HG + 3, :], ALU.mult).then_inc(mod_up, 1)
            v.wait_ge(g2_in, 16)
            m8 = mod[:, 8:10, :].rearrange("p n e -> p (n e)")
            V.tensor_tensor(m8, m8, g2[:], ALU.mult).then_inc(mod_up, 1)
            v.wait_ge(mod_up, 2)

            def second_norm(t):
                v.wait_ge(h2_r, t + 1)
                if t >= 2:
                    v.wait_ge(h2_out[t % 2], 16 * (t // 2))
                    v.wait_ge(h2_T, t - 1)
                V.scalar_tensor_tensor(h2[:, t % 2, :], X[:, t, :], rstd[:, t:t + 1], m8,
                                       ALU.mult, ALU.mult).then_inc(h2_m, 1)

            for t in range(T):
                v.wait_ge(y_mm, t + 1)
                if t >= 2:
                    v.wait_ge(x2_up, t - 1)
                V.tensor_tensor(ytmp[:, t % 2, :],
                                PS[:, t % 2 * 2:t % 2 * 2 + 2, :].rearrange("p b e -> p (b e)"),
                                mod[:, 4:6, :].rearrange("p n e -> p (n e)"),
                                ALU.mult).then_inc(y_gated, 1)
                second_norm(t)
                if t >= 1:
                    v.wait_ge(rt_mm, t)
                    V.tensor_tensor(logits[:, t - 1, :], PS[:, 6, 0:G + E_ALL], rbias[:],
                                    ALU.add).then_inc(rt_out, 1)
            v.wait_ge(rt_mm, T)
            V.tensor_tensor(logits[:, T - 1, :], PS[:, 6, 0:G + E_ALL], rbias[:],
                            ALU.add).then_inc(rt_out, 1)

            v.wait_ge(rt_out, T)
            v.wait_ge(iota_up, 1)
            v.wait_ge(h2T_up, T)
            v.wait_ge(x2_sq, T)

            def wide(ap, n):
                return ap.unsqueeze(2).broadcast_to([P, T, n])

            def first_best(oh, val, best):
                step(V.tensor_tensor(eqv[:], val, wide(best[:], 4), ALU.is_equal))
                step(V.tensor_tensor(eqv[:], eqv[:], first4[:].unsqueeze(1).broadcast_to([P, T, 4]),
                                     ALU.mult))
                step(V.tensor_reduce(fst[:], eqv[:], AX.X, ALU.max))
                step(V.tensor_tensor(oh[:], first4[:].unsqueeze(1).broadcast_to([P, T, 4]),
                                     wide(fst[:], 4), ALU.is_equal))

            gl, xl = logits[:, :, 0:G], logits[:, :, G:]
            step(V.tensor_reduce(gmax[:], gl, AX.X, ALU.max))
            V.tensor_tensor(gdif[:], gl, wide(gmax[:], G), ALU.subtract).then_inc(r_exp_in, 1)
            first_best(oh_g, gl, gmax)
            for g in range(G):
                m = V.tensor_tensor(picked[:, :, :, g], xl[:, :, g * EG:(g + 1) * EG],
                                    oh_g[:, :, g:g + 1].broadcast_to([P, T, EG]), ALU.mult)
            step(m)
            step(V.tensor_reduce(local[:], picked[:], AX.X, ALU.add))
            step(V.tensor_reduce(lmax[:], local[:], AX.X, ALU.max))
            first_best(oh_1, local[:], lmax)
            step(V.scalar_tensor_tensor(local2[:], oh_1[:], -1e30, local[:], ALU.mult, ALU.add))
            step(V.tensor_reduce(lmax2[:], local2[:], AX.X, ALU.max))
            first_best(oh_2, local2[:], lmax2)
            V.tensor_tensor(ldif[:], lmax2[:], lmax[:], ALU.subtract).then_inc(r_exp_in, 1)
            for mk, oh in ((m1, oh_1), (m2, oh_2)):
                for g in range(G):
                    m = V.tensor_tensor(mk[:, :, g, :], oh[:],
                                        oh_g[:, :, g:g + 1].broadcast_to([P, T, EG]), ALU.mult)
            step(m)
            flat = lambda ap: ap.rearrange("p t g e -> p t (g e)")
            V.tensor_tensor(both[:], flat(m1[:]), flat(m2[:]), ALU.add).then_inc(masks_up, 1)
            v.wait_ge(r_exp, 2)
            step(V.tensor_reduce(gsum[:], gexp[:], AX.X, ALU.add))
            step(V.reciprocal(pgroup[:], gsum[:]))
            step(V.tensor_scalar(lden[:], lexp[:], 1.0, None, ALU.add))
            step(V.reciprocal(lrec[:], lden[:]))
            step(V.tensor_tensor(w12[:, 0, :], pgroup[:], lrec[:], ALU.mult))
            step(V.tensor_tensor(w12[:, 1, :], w12[:, 0, :], lexp[:], ALU.mult))
            v.wait_ge(rank_mm, 1)
            te = lambda ap: ap.rearrange("p (t e) -> p t e", e=E_ALL)
            step(V.tensor_copy(tot[:], te(PS[:, 1, 0:T * E_ALL])))
            step(V.memset(run[:, 0, :], 0.0))
            for t in range(T):
                step(V.tensor_tensor(run[:, t + 1, :], run[:, t, :], tot[:, t, :], ALU.add))
            step(V.tensor_tensor(rank[:], te(PS[:, 0, 0:T * E_ALL]), run[:, 0:T, :], ALU.add))
            step(V.tensor_tensor(hund[:], run[:, T, :].unsqueeze(2).broadcast_to([P, E_ALL, T]),
                                 step128[:].unsqueeze(1).broadcast_to([P, E_ALL, T]), ALU.is_gt))
            step(V.tensor_reduce(ntile[:], hund[:], AX.X, ALU.add))
            step(V.tensor_tensor_scan(tend[:], ones[:, 0:E_ALL], ntile[:], 0.0, ALU.mult, ALU.add))
            step(V.tensor_tensor(tbase[:], tend[:], ntile[:], ALU.subtract))
            step(V.scalar_tensor_tensor(pos[:], tbase[:].unsqueeze(1).broadcast_to([P, T, E_ALL]),
                                        float(P), rank[:], ALU.mult, ALU.add))
            for n, mk in enumerate((m1, m2)):
                step(V.tensor_tensor(pick[:], pos[:], flat(mk[:]), ALU.mult))
                step(V.tensor_reduce(slots[:, n, :], pick[:], AX.X, ALU.add))
            step(V.tensor_copy(slots_i[:], slots[:]))
            flat_i = slots_i[:].rearrange("p n t -> p (n t)")
            step(V.tensor_scalar(slot_lo[:], flat_i, P - 1, None, ALU.bitwise_and))
            step(V.tensor_scalar(slot_hi[:], flat_i, 7, None, ALU.logical_shift_right))
            step(V.tensor_copy(slot_lane[:], slot_lo[:]))
            step(V.tensor_copy(slot_tile[:], slot_hi[:]))
            nt = lambda ap, n: ap.unsqueeze(2).broadcast_to([P, 2 * T, n])
            V.tensor_tensor(lanes[:], lane[:].unsqueeze(1).broadcast_to([P, 2 * T, P]),
                            nt(slot_lane[:], P), ALU.is_equal)
            step(V.tensor_tensor(in_tile[:], tile_no[:].unsqueeze(1).broadcast_to([P, 2 * T, TILES]),
                                 nt(slot_tile[:], TILES), ALU.is_equal))
            V.tensor_tensor(tiles[:, :, 0:TILES], in_tile[:],
                            nt(token_row[:].rearrange("p n t -> p (n t)"), TILES), ALU.mult)
            V.tensor_tensor(tiles[:, :, TILES:2 * TILES], in_tile[:],
                            nt(w12[:].rearrange("p n t -> p (n t)"), TILES),
                            ALU.mult).then_inc(onehot_up, 1)
            step(V.tensor_tensor(t_cmp[:], tend[:].unsqueeze(1).broadcast_to([P, TILES, E_ALL]),
                                 tile_no[:].unsqueeze(2).broadcast_to([P, TILES, E_ALL]),
                                 ALU.is_le))
            step(V.tensor_reduce(t_exp[:], t_cmp[:], AX.X, ALU.add))
            step(V.tensor_scalar(t_exp[:], t_exp[:], float(E_ALL - 1), None, ALU.min))
            step(V.memset(t_new[:, 0:1], 1.0))
            step(V.tensor_tensor(t_new[:, 1:TILES], t_exp[:, 1:TILES], t_exp[:, 0:TILES - 1],
                                 ALU.not_equal))
            for dst, src in ((t_exp_i, t_exp), (t_new_i, t_new)):
                V.tensor_copy(dst[:, 0:TILES:2], src[:, 0:EVENS])
                m = V.tensor_copy(dst[:, 1:TILES:2], src[:, EVENS:TILES])
            m.then_inc(tiles_up, 1)
            v.wait_ge(table_mm, 1)
            step(V.memset(slot_row[:, TILES:TILES + 1], 0))
            step(V.tensor_copy(row_plus[:], PS[:, 2, 0:TILES]))
            step(V.tensor_scalar(unused[:], row_plus[:], 0.0, unused_row[:, 0:1], ALU.is_equal,
                                 ALU.mult))
            for s, part in ((0, slice(0, EVENS)), (1, slice(EVENS, TILES))):
                step(V.scalar_tensor_tensor(slot_row[:, s:TILES:2], row_plus[:, part], -1.0,
                                            unused[:, part], ALU.add, ALU.add))
                m = V.tensor_copy(slot_w[:, s:TILES:2],
                                  PS[:, 2, TILES + part.start:TILES + part.stop])
            m.then_inc(table_up, 1)
            v.wait_ge(table_up, 1)

            def less_hi(dst, src, hi):
                return V.tensor_tensor(dst, src, hi.bitcast(F32), ALU.subtract)

            def lo_chunk(j, c, s):
                v.wait_ge(hi_up, CHUNKS * j + c + 1)
                less_hi(w_lo[:, c % RING], weights(c, s), w_hi[:, c % RING]).then_inc(lo_dve, 1)

            def x_lo(j, half):
                v.wait_ge(xT_hi, 2 * j + half + 1)
                flat = lambda ap: ap[:, 4 * half:4 * half + 4, :].rearrange("p k q -> p (k q)")
                less_hi(flat(XT_lo), PS[:, half, :], flat(XT_hi)).then_inc(xT_lo, 1)

            def y_tile(i, s):
                j = 2 * i + s
                v.wait_ge(chunk_mm, CHUNKS * j + CHUNKS)
                if not isinstance(i, int) or i >= 1:
                    v.wait_ge(y_out[s], 16 * i)
                V.tensor_copy(row_out[:, s:s + 1], slot_row[:, bass.ds(j, 1)])
                V.scalar_tensor_tensor(Y[:, s, :], PS[:, 5:7, :].rearrange("p b e -> p (b e)"),
                                       slot_w[:, bass.ds(j, 1)], g2v, ALU.mult,
                                       ALU.mult).then_inc(y_up, 1)

            def expert(i, s, first, last):
                j = 2 * i + s
                lo_chunk(j, 4, s)
                lo_chunk(j, 5, s)
                if not first:
                    y_tile(i - 1 + s, 1 - s)
                lo_chunk(j, 6, s)
                for c in range(8, CHUNKS - 1):
                    lo_chunk(j, c, s)
                v.wait_ge(chunk_mm, CHUNKS * j + 8)
                v.wait_ge(sil_up, j + 1)
                if not first:
                    v.wait_ge(hT_mm, j)
                V.tensor_tensor(hid[:], PS[:, 3, :], sil[:], ALU.mult).then_inc(hid_up, 1)
                if not last:
                    x_lo(j + 1, 0)
                v.wait_ge(hT_hi, j + 1)
                less_hi(hidT_lo[:].rearrange("p k q -> p (k q)"), PS[:, 4, :],
                        hidT_hi[:].rearrange("p k q -> p (k q)")).then_inc(hT_lo, 1)
                if not last:
                    x_lo(j + 1, 1)
                    rows_of(j, s, i)
                    for c in range(3):
                        lo_chunk(j + 1, c, 1 - s)

            g2v = mod[:, 10:12, :].rearrange("p n e -> p (n e)")

            def rows_of(j, s, i):
                v.wait_ge(xg_in[s], 16 * i + 16)
                V.tensor_copy(row_in[:, s:s + 1], slot_row[:, bass.ds(j + 2, 1)])                    .then_inc(row_in_up, 1)

            for s in range(2):
                V.tensor_copy(row_in[:, s:s + 1], slot_row[:, s:s + 1]).then_inc(row_in_up, 1)
            for half in range(2):
                x_lo(0, half)
            for c in range(3):
                lo_chunk(0, c, 0)
            expert(0, 0, True, False)
            expert(0, 1, False, False)
            with v.Fori(1, TILES // 2) as i:
                for s in range(2):
                    expert(i, s, False, False)
            expert(TILES // 2, 0, False, True)
            y_tile(TILES // 2, 0)
            v.wait_ge(gf_in, 16)
            for t in range(T):
                v.wait_ge(x3_r, t + 1)
                if t >= 2:
                    v.wait_ge(fin_out[t % 2], 16 * (t // 2))
                V.scalar_tensor_tensor(fin[:, t % 2, :], X[:, t, :], rstd[:, t:t + 1], gf[:],
                                       ALU.mult, ALU.mult).then_inc(fin_up, 1)

        @block.gpsimd
        def _(pool):
            G_ = nc.gpsimd
            step = Chain(pool, pool_step)

            def select(ap, pattern, base, cm, op=ALU.is_ge, fill=0.0):
                return G_.affine_select(out=ap, in_=ap, pattern=pattern, compare_op=op, fill=fill,
                                        base=base, channel_multiplier=cm)

            G_.memset(ones[:], 1.0)
            G_.memset(causal[:], 0.0)
            G_.memset(level_mask[:].rearrange("p l t -> p (l t)"), 0.0)
            G_.memset(pool_w[:].rearrange("p l t -> p (l t)"), 0.0)
            G_.memset(power[:], -0.5)
            G_.memset(before[:], 1.0)
            step(G_.memset(ident[:], 0.0))
            select(ident[:], [[-1, P]], 0, 1, ALU.not_equal, 1.0)
            select(before[:], [[1, P]], -1, -1)
            step(select(causal[:], [[-1, P]], 0, 1, fill=-1e30))
            for lv in range(LEVELS):
                half = P >> (lv + 1)
                m = level_mask[:, lv, :].rearrange("p (n h t) -> p n h t", h=2, t=half)[:, :, 1, :]
                n = P // (2 * half)
                step(G_.memset(m, 1.0))
                step(select(m, [[-2 * half, n], [0, half]], 0, 1))
                step(select(m, [[2 * half, n], [0, half]], half - 1, -1))
            for b in range(2):
                for h in range(2):
                    w = 2 << (2 * b + h)
                    r = slice(HD * h, HD * (h + 1))
                    step(G_.memset(wcol[r, b:b + 1], float(w)))
                    step(G_.memset(iwcol[r, b:b + 1], 1.0 / w))
                    step(G_.iota(invc[r, b, :], [[1, 16]], base=1, channel_multiplier=0,
                                allow_small_or_imprecise_dtypes=True))
            for b in range(2):
                m = G_.tensor_scalar(invc[:, b, :], invc[:, b, :], wcol[:, b:b + 1], None, ALU.min)
            step(m)
            G_.memset(VA[:, :, NH * (HD + 1):VP], 0.0)
            G_.memset(VA[:, :, 0:NH * (HD + 1)].rearrange("p t (h d) -> p t h d", h=NH)
                      [:, :, :, HD:HD + 1].rearrange("p t h d -> p t (h d)"), 1.0)\
                .then_inc(consts, 1)
            for t in range(T):
                pool.wait_ge(x_sq, t + 1)
                step(G_.tensor_scalar(ms[:, t:t + 1], ss[:, t:t + 1], 1.0 / D, EPS, ALU.mult,
                                      ALU.add))
                step(G_.tensor_tensor(rstd[:, t:t + 1], ms[:, t:t + 1], power[:, 0:1], ALU.pow))
                G_.tensor_scalar(xhat[:, t, :], X[:, t, :], rstd[:, t:t + 1], None, ALU.mult)\
                    .then_inc(x_hat, 1)
            pool.wait_ge(pt_act, NB)
            pool.wait_ge(pt_dve, NB)
            for j in range(3):
                G_.tensor_scalar(PT[:, B_FQ + j, :], PT[:, B_FQ + j, :], float(HD) ** -0.5, None,
                                 ALU.mult).then_inc(q_scaled, 1)
            pool.wait_ge(q_scaled, 3)
            for e in range(2):
                for rows in (QA[e], KA[e]):
                    step(G_.memset(rows[HD:P, :], 0.0))
                    step(G_.memset(rows[HD:HD + 2, :], 1.0))
            G_.memset(head_ms[:, 0, 0:32], -1.0).then_inc(q_scaled, 1)
            pool.wait_ge(q_scaled, 4)
            for b in range(2):
                step(G_.tensor_tensor(invc[:, b, :], invc[:, b, :], head_ms[:, 0, 0:16], ALU.pow))
            for b in range(2):
                u = PT[:, B_PU + b, :]
                src, width, dst = u, 1, 0
                for d in range(2 * b + 2):
                    if d == 2 * b + 1:
                        rows = slice(HD, P)
                    else:
                        rows = slice(0, P)
                    o = win_sum[rows, dst, :]
                    step(G_.tensor_copy(o[:, 0:width], src[rows, 0:width]))
                    step(G_.tensor_tensor(o[:, width:S], src[rows, width:S],
                                          src[rows, 0:S - width], ALU.add))
                    if rows == slice(HD, P):
                        last = dst
                    src, width, dst = win_sum[:, dst, :], 2 * width, 1 - dst
                for h, buf in ((0, 1 - last), (1, last)):
                    r = slice(HD * h, HD * (h + 1))
                    w = win_sum[r, buf, :]
                    step(G_.tensor_tensor(w[:, 0:16], w[:, 0:16], invc[r, b, :], ALU.mult))
                    step(G_.tensor_scalar(w[:, 16:S], w[:, 16:S], iwcol[r, b:b + 1], None, ALU.mult))
                    step(G_.tensor_tensor(PT[r, B_PU + b, :], w, PT[r, B_PU + b, :], ALU.subtract))
                G_.memset(head_ms[:, 0, 32:33], 0.0).then_inc(pooled_up, 1)

            def hgrn_pair(i, first):
                if first:
                    pool.wait_ge(silu_up, 3)
                    pool.wait_ge(s_done, 16 * PAIRS)
                    pool.wait_ge(pool_out, 1)
                else:
                    pool.wait_ge(lv_mm, 16 * i)
                G_.tensor_copy(qb[:], PT[:, B_HQ + i, :]).then_inc(q_up, 1)
                pool.wait_ge(q_up, i + 1)
                pool.wait_ge(kd_e, i + 1)
                G_.tensor_tensor(dec[:, 0, :], dec[:, 0, :], kb[:], ALU.mult).then_inc(kd_up, 1)
                for lv in range(LEVELS):
                    pool.wait_ge(e_up, LEVELS * i + lv + 1)
                    if not first or lv >= 2:
                        pool.wait_ge(lv_mm, 16 * i + 2 * lv)
                    half = P >> (lv + 1)
                    cut = lambda ap: ap.rearrange("p (n h t) -> p n h t", h=2, t=half)
                    d, g = cut(dec[:, (lv + 1) % 2, :]), cut(gk[:, lv % 2, :])
                    G_.tensor_tensor(g[:, :, 1, :], d[:, :, 1, :], cut(qb[:])[:, :, 1, :], ALU.mult)
                    G_.tensor_tensor(d[:, :, 0, :], d[:, :, 0, :], cut(kb[:])[:, :, 0, :],
                                     ALU.mult).then_inc(g_up, 1)
                    if lv == 0:
                        pool.wait_ge(qe_exp, i + 1)
                        G_.tensor_tensor(qe[:], qe[:], qb[:], ALU.mult).then_inc(qe_up, 1)

            hgrn_pair(0, True)
            with pool.Fori(1, PAIRS) as i:
                hgrn_pair(i, False)
            for g in range(2):
                pool.wait_ge(fss, g + 1)
                step(G_.tensor_scalar(head_ms[:, g, :], head_ss[:, g, :], 1.0 / HD, EPS, ALU.mult,
                                      ALU.add))
                G_.tensor_tensor(head_r[:, g, :], head_ms[:, g, :], power[:, 0:T * NH],
                                 ALU.pow).then_inc(frs, 1)
            pool.wait_ge(ho_mm, PAIRS)
            pool.wait_ge(on_up, 2)
            pool.wait_ge(mT_mm, 4 * PAIRS)
            step(G_.memset(rw[:].rearrange("p l t -> p (l t)"), 0.0))
            pool.dma_start(rw[:, :, 0:G], a["router_group_w"][0].rearrange("(k p) e -> p k e", p=P),
                           allow_slow_non_contiguous=True).then_inc(rw_in, 16)
            pool.dma_start(rw[:, :, G:G + E_ALL],
                           a["router_expert_w"][0].rearrange("(k p) e -> p k e", p=P),
                           allow_slow_non_contiguous=True).then_inc(rw_in, 16)
            G_.memset(zero_rows[:], 0.0).then_inc(zero_up, 1)
            pool.dma_start(g2[:], a["norm2_g"].partition_broadcast(P).rearrange("p a e -> p (a e)"))\
                .then_inc(g2_in, 16)

            for t in range(T):
                pool.wait_ge(y_gated, t + 1)
                G_.tensor_tensor(X[:, t, :], X[:, t, :], ytmp[:, t % 2, :], ALU.add)\
                    .then_inc(x2_up, 1)
                pool.wait_ge(x2_sq, t + 1)
                step(G_.tensor_scalar(ms[:, t:t + 1], ss[:, t:t + 1], 1.0 / D, EPS, ALU.mult,
                                      ALU.add))
                G_.tensor_tensor(rstd[:, t:t + 1], ms[:, t:t + 1], power[:, 0:1],
                                 ALU.pow).then_inc(h2_r, 1)
                pool.wait_ge(h2_m, t + 1)
                G_.tensor_tensor(h2[:, t % 2, :], h2[:, t % 2, :],
                                 mod[:, 6:8, :].rearrange("p n e -> p (n e)"),
                                 ALU.add).then_inc(h2_up, 1)
            pool.wait_ge(h2_T, T)
            pool.wait_ge(rt_mm, T)
            pool.wait_ge(y_gated, T)
            for s in range(2):
                pool.wait_ge(h2_out[s], 16 * T // 2)
            G_.iota(token_row[:], [[0, 2], [P, T]], base=1, channel_multiplier=1,
                    allow_small_or_imprecise_dtypes=True)
            G_.iota(lane[:], [[1, P]], base=0, channel_multiplier=0,
                    allow_small_or_imprecise_dtypes=True)
            G_.iota(unused_row[:], [[0, 1]], base=S + 1, channel_multiplier=1,
                    allow_small_or_imprecise_dtypes=True)
            G_.memset(tiles[:].rearrange("p n t -> p (n t)"), 0.0)
            G_.iota(tile_no[:], [[1, TILES]], base=0, channel_multiplier=0,
                    allow_small_or_imprecise_dtypes=True)
            G_.iota(step128[:], [[P, T]], base=0, channel_multiplier=0,
                    allow_small_or_imprecise_dtypes=True)
            G_.iota(first4[:], [[-1, 4]], base=4, channel_multiplier=0,
                    allow_small_or_imprecise_dtypes=True).then_inc(iota_up, 1)
            def gather(j, s, n, first):
                if not first:
                    pool.wait_ge(xT_mm, 2 * j - 2)
                    pool.wait_ge(gathers, j - 1)
                pool.wait_ge(row_in_up, j + 1)
                G_.tensor_tensor(waited_pool[:, s:s + 1], power[:, 0:1], power[:, 1:2],
                                 ALU.mult).then_inc(gathers, 1)
                pool.indirect_dma_start(
                    out=XG[:, s, :], out_offset=None, in_=h2_rows,
                    in_offset=bass.IndirectOffsetOnAxis(ap=row_in[:, s:s + 1], axis=0))                    .then_inc(xg_in[s], 16)

            def scatter(j, s, n):
                pool.wait_ge(y_up, j + 1)
                if n is not None:
                    pool.wait_ge(y_out[1 - s], 16 * n)
                if not isinstance(j, int) or j >= 2:
                    pool.wait_ge(scatters, j - 1)
                G_.tensor_tensor(waited_pool[:, 2 + s:3 + s], power[:, 0:1], power[:, 1:2],
                                 ALU.mult).then_inc(scatters, 1)
                pool.indirect_dma_start(
                    out=acc_rows, out_offset=bass.IndirectOffsetOnAxis(
                        ap=row_out[:, s:s + 1], axis=0),
                    in_=Y[:, s, :], in_offset=None, compute_op=ALU.add).then_inc(y_out[s], 16)

            pool.wait_ge(x2_out, 16 * T)
            pool.wait_ge(unused_out, 32)
            for s in range(2):
                pool.wait_ge(h2_out[s], 16 * T // 2)
            def lo_chunk(j, c, s):
                pool.wait_ge(hi_up, CHUNKS * j + c + 1)
                G_.tensor_tensor(w_lo[:, c % RING], weights(c, s), w_hi[:, c % RING].bitcast(F32),
                                 ALU.subtract).then_inc(lo_pool, 1)

            def expert(i, s, first, last):
                j = 2 * i + s
                lo_chunk(j, 7, s)
                if not first:
                    scatter(j - 1, 1 - s, i if not isinstance(j, int) or j >= 2 else None)
                if not last:
                    gather(j + 2, s, i + 1, False)
                lo_chunk(j, 11, s)
                if last != 2:
                    lo_chunk(j + 1, 3, 1 - s)

            gather(0, 0, 0, True)
            gather(1, 1, 0, True)
            lo_chunk(0, 3, 0)
            expert(0, 0, True, 0)
            expert(0, 1, False, 0)
            with pool.Fori(1, TILES // 2 - 1) as i:
                for s in range(2):
                    expert(i, s, False, 0)
            expert(TILES // 2 - 1, 0, False, 0)
            expert(TILES // 2 - 1, 1, False, 1)
            expert(TILES // 2, 0, False, 2)
            scatter(TILES - 1, 0, TILES // 2)
            for t in range(T):
                pool.wait_ge(x3_sq, t + 1)
                step(G_.tensor_scalar(ms[:, t:t + 1], ss[:, t:t + 1], 1.0 / D, EPS, ALU.mult,
                                      ALU.add))
                G_.tensor_tensor(rstd[:, t:t + 1], ms[:, t:t + 1], power[:, 0:1],
                                 ALU.pow).then_inc(x3_r, 1)


_INS = ['x', 'c', 'w_ada', 'b_ada', 'norm1_g', 'w_in', 'fox_f_bias', 'fox_norm_g', 'hgrn_lb_logits',
        'hgrn_norm_g', 'pool_w', 'pool_scale', 'w_out', 'norm2_g', 'router_group_w',
        'router_group_b', 'router_expert_w', 'router_expert_b', 'expert_w_gate', 'expert_w_up',
        'expert_w_down', 'final_norm_g']


def kernel(**inputs):
    import numpy as _np
    import concourse.bacc as _bacc
    from concourse.bass_utils import run_bass_kernel_spmd as _run

    nc = _bacc.Bacc("TRN2", target_bir_lowering=False, num_devices=1)
    arrays, aps = {}, {}
    for name in _INS:
        v = _np.ascontiguousarray(inputs[name])
        arrays[f"in_{name}"] = v
        aps[name] = nc.dram_tensor(f"in_{name}", v.shape, mybir.dt.from_np(v.dtype),
                                   kind="ExternalInput").ap()
    out = nc.dram_tensor("out", (1, S, D), F32, kind="ExternalOutput").ap()
    build(nc, aps, out)
    r = _run(nc, [arrays], core_ids=[0])
    return r.results[0]["out"]
```
